# Optimizing a Trainium2 kernel written in Bass

```python
import jax, jax.numpy as jnp
from jax import lax
import numpy as np

D_MODEL = 1024
BATCH = 1
SEQ = 1024
DEPTH = 1
DEC_BATCH = 8
DEC_SEQ = 1
PAST_LEN = 8192
PAGE_SIZE = 128

N_MEM = 256
D_MIX = D_MODEL
D_CONV = D_MIX // 2
D_GLA = D_MIX - D_CONV
CONV_W = 31
GLA_HEADS = 4
GLA_DK = D_GLA // 2 // GLA_HEADS
GLA_DV = D_GLA // GLA_HEADS
GLA_RANK = 16
GLA_TAU = 16.0
GLA_CHUNK = 16
XA_HEADS = 4
XA_HD = D_MODEL // XA_HEADS
D_FF = 4 * D_MODEL
EPS = 1e-6
D_IN = 2 * D_CONV + 2 * GLA_HEADS * GLA_DK + GLA_HEADS * GLA_DV + D_GLA + GLA_RANK

kernel_name = 'hybrid_conformer_gla_xattn_decoder_step'

def rms_norm(x, g):
    xf = x.astype(jnp.float32)
    y = xf * lax.rsqrt(jnp.mean(xf * xf, axis=-1, keepdims=True) + EPS)
    return (y * g.astype(jnp.float32)).astype(x.dtype)

def layer_norm(x, g, b):
    xf = x.astype(jnp.float32)
    mu = jnp.mean(xf, axis=-1, keepdims=True)
    xc = xf - mu
    y = xc * lax.rsqrt(jnp.mean(xc * xc, axis=-1, keepdims=True) + EPS)
    return (y * g.astype(jnp.float32) + b.astype(jnp.float32)).astype(x.dtype)

def conformer_conv(u, prefix, w_dw, b_dw, ln_g, ln_b):
    full = jnp.concatenate([prefix.astype(u.dtype), u], axis=1)
    y = lax.conv_general_dilated(
        full, w_dw.astype(u.dtype)[:, None, :], window_strides=(1,), padding='VALID',
        dimension_numbers=('NWC', 'WIO', 'NWC'), feature_group_count=D_CONV)
    y = jax.nn.silu(layer_norm(y + b_dw, ln_g, ln_b))
    return y, full[:, -(CONV_W - 1):]

def gla_chunked(q, k, v, log_a, s0):
    B, T = q.shape[0], q.shape[1]
    n = -(-T // GLA_CHUNK)
    pad = n * GLA_CHUNK - T

    def blocks(t):
        t = jnp.pad(t.astype(jnp.float32), ((0, 0), (0, pad), (0, 0), (0, 0)))
        return t.reshape(B, n, GLA_CHUNK, t.shape[2], t.shape[3])

    q, k, v, log_a = blocks(q), blocks(k), blocks(v), blocks(log_a)
    b = jnp.cumsum(log_a, axis=2)
    causal = jnp.tril(jnp.ones((GLA_CHUNK, GLA_CHUNK), dtype=bool))
    diff = b[:, :, :, None] - b[:, :, None]
    decay = jnp.exp(jnp.where(causal[:, :, None, None], diff, -jnp.inf))
    scores = jnp.einsum('bnihd,bnjhd,bnijhd->bnhij', q, k, decay)
    o_intra = jnp.einsum('bnhij,bnjhv->bnihv', scores, v)

    b_last = b[:, :, -1]
    q_in = q * jnp.exp(b)
    k_in = k * jnp.exp(b_last[:, :, None] - b)
    chunk_kv = jnp.einsum('bnjhd,bnjhv->bnhdv', k_in, v)

    def step(S, xs):
        qc, dec, kv = xs
        o = jnp.einsum('bihd,bhdv->bihv', qc, S)
        S = jnp.exp(dec)[..., None] * S + kv
        return S, o

    S, o_inter = lax.scan(step, s0.astype(jnp.float32),
                          (jnp.moveaxis(q_in, 1, 0), jnp.moveaxis(b_last, 1, 0),
                           jnp.moveaxis(chunk_kv, 1, 0)))
    o = o_intra + jnp.moveaxis(o_inter, 0, 1)
    o = o.reshape(B, n * GLA_CHUNK, o.shape[3], o.shape[4])[:, :T]
    return o, S

def token_mix(h, conv_prefix, s0, w_in, w_alpha, b_alpha, w_dw, b_dw, ln_g, ln_b,
              gla_g, w_out):
    B, T, _ = h.shape
    proj = h @ w_in
    i1 = D_CONV
    i2 = 2 * D_CONV
    i3 = i2 + GLA_HEADS * GLA_DK
    i4 = i3 + GLA_HEADS * GLA_DK
    i5 = i4 + GLA_HEADS * GLA_DV
    i6 = i5 + D_GLA
    c_val, c_gate, q, k, v, r, a_lr = jnp.split(proj, [i1, i2, i3, i4, i5, i6], axis=-1)
    u = c_val * jax.nn.sigmoid(c_gate)
    conv_out, conv_state = conformer_conv(u, conv_prefix, w_dw, b_dw, ln_g, ln_b)
    log_a = jax.nn.log_sigmoid((a_lr @ w_alpha + b_alpha).astype(jnp.float32)) / GLA_TAU
    o, s_new = gla_chunked(
        q.reshape(B, T, GLA_HEADS, GLA_DK) * (GLA_DK ** -0.5),
        k.reshape(B, T, GLA_HEADS, GLA_DK),
        v.reshape(B, T, GLA_HEADS, GLA_DV),
        log_a.reshape(B, T, GLA_HEADS, GLA_DK), s0)
    o = rms_norm(o, gla_g).astype(h.dtype).reshape(B, T, D_GLA) * jax.nn.silu(r)
    out = jnp.concatenate([conv_out, o], axis=-1) @ w_out
    return out, conv_state, s_new

def memory_kv(mem, g, w_k, w_v):
    B = mem.shape[0]
    m = rms_norm(mem, g)
    mk = (m @ w_k).reshape(B, N_MEM, XA_HEADS, XA_HD)
    mv = (m @ w_v).reshape(B, N_MEM, XA_HEADS, XA_HD)
    return mk, mv

def cross_attn(h, mk, mv, w_q, w_o):
    B, T, _ = h.shape
    q = (h @ w_q).reshape(B, T, XA_HEADS, XA_HD)
    s = jnp.einsum('bthd,bmhd->bhtm', q, mk).astype(jnp.float32) * (XA_HD ** -0.5)
    p = jax.nn.softmax(s, axis=-1).astype(mv.dtype)
    o = jnp.einsum('bhtm,bmhd->bthd', p, mv).reshape(B, T, D_MODEL)
    return o @ w_o

def setup_inputs(seed: int = 0) -> dict:
    key = jax.random.key(seed)
    ks = jax.random.split(key, 32)
    f32 = jnp.float32

    def nrm(k, shape, scale):
        return scale * jax.random.normal(k, shape, f32)

    return {
        'x_prompt': nrm(ks[0], (BATCH, SEQ, D_MODEL), 1.0),
        'x_sample': nrm(ks[1], (DEC_BATCH, DEC_SEQ, D_MODEL), 1.0),
        'cache_conv': nrm(ks[2], (DEPTH, DEC_BATCH, CONV_W - 1, D_CONV), 0.5),
        'state_gla': nrm(ks[3], (DEPTH, DEC_BATCH, GLA_HEADS, GLA_DK, GLA_DV), 1.0),
        'cache_mem_k': nrm(ks[4], (DEPTH, DEC_BATCH, N_MEM, XA_HEADS, XA_HD), 1.0),
        'cache_mem_v': nrm(ks[5], (DEPTH, DEC_BATCH, N_MEM, XA_HEADS, XA_HD), 1.0),
        'mem_prompt': nrm(ks[6], (BATCH, N_MEM, D_MODEL), 1.0),
        'norm_mix_g': 1.0 + nrm(ks[7], (DEPTH, D_MODEL), 0.02),
        'w_in': nrm(ks[8], (DEPTH, D_MODEL, D_IN), D_MODEL ** -0.5),
        'w_alpha': nrm(ks[9], (DEPTH, GLA_RANK, GLA_HEADS * GLA_DK), GLA_RANK ** -0.5),
        'b_alpha': nrm(ks[10], (DEPTH, GLA_HEADS * GLA_DK), 0.1),
        'w_dw': nrm(ks[11], (DEPTH, CONV_W, D_CONV), CONV_W ** -0.5),
        'b_dw': nrm(ks[12], (DEPTH, D_CONV), 0.02),
        'conv_ln_g': 1.0 + nrm(ks[13], (DEPTH, D_CONV), 0.02),
        'conv_ln_b': nrm(ks[14], (DEPTH, D_CONV), 0.02),
        'gla_norm_g': 1.0 + nrm(ks[15], (DEPTH, GLA_DV), 0.02),
        'w_out': nrm(ks[16], (DEPTH, D_MIX, D_MODEL), D_MIX ** -0.5),
        'norm_xa_g': 1.0 + nrm(ks[17], (DEPTH, D_MODEL), 0.02),
        'mem_norm_g': 1.0 + nrm(ks[18], (DEPTH, D_MODEL), 0.02),
        'w_xq': nrm(ks[19], (DEPTH, D_MODEL, D_MODEL), D_MODEL ** -0.5),
        'w_xk': nrm(ks[20], (DEPTH, D_MODEL, D_MODEL), D_MODEL ** -0.5),
        'w_xv': nrm(ks[21], (DEPTH, D_MODEL, D_MODEL), D_MODEL ** -0.5),
        'w_xo': nrm(ks[22], (DEPTH, D_MODEL, D_MODEL), D_MODEL ** -0.5),
        'norm_ffn_g': 1.0 + nrm(ks[23], (DEPTH, D_MODEL), 0.02),
        'w_up': nrm(ks[24], (DEPTH, D_MODEL, D_FF), D_MODEL ** -0.5),
        'w_down': nrm(ks[25], (DEPTH, D_FF, D_MODEL), D_FF ** -0.5),
        'final_g': 1.0 + nrm(ks[26], (D_MODEL,), 0.02),
    }

def reference(x_prompt, x_sample, cache_conv, state_gla, cache_mem_k, cache_mem_v,
              mem_prompt, norm_mix_g, w_in, w_alpha, b_alpha, w_dw, b_dw, conv_ln_g,
              conv_ln_b, gla_norm_g, w_out, norm_xa_g, mem_norm_g, w_xq, w_xk, w_xv,
              w_xo, norm_ffn_g, w_up, w_down, final_g):

    def run_layer(x, l, conv_prefix, s0, mk, mv):
        m, conv_state, s_new = token_mix(
            rms_norm(x, norm_mix_g[l]), conv_prefix, s0, w_in[l], w_alpha[l], b_alpha[l],
            w_dw[l], b_dw[l], conv_ln_g[l], conv_ln_b[l], gla_norm_g[l], w_out[l])
        x = x + m
        x = x + cross_attn(rms_norm(x, norm_xa_g[l]), mk, mv, w_xq[l], w_xo[l])
        h = rms_norm(x, norm_ffn_g[l])
        x = x + jnp.square(jax.nn.relu(h @ w_up[l])) @ w_down[l]
        return x, conv_state, s_new

    xp = x_prompt
    conv_p, gla_p, mk_p, mv_p = [], [], [], []
    for l in range(DEPTH):
        mk, mv = memory_kv(mem_prompt, mem_norm_g[l], w_xk[l], w_xv[l])
        prefix0 = jnp.zeros((xp.shape[0], CONV_W - 1, D_CONV), xp.dtype)
        s00 = jnp.zeros((xp.shape[0], GLA_HEADS, GLA_DK, GLA_DV), jnp.float32)
        xp, cs, ss = run_layer(xp, l, prefix0, s00, mk, mv)
        conv_p.append(cs)
        gla_p.append(ss)
        mk_p.append(mk)
        mv_p.append(mv)
    y_prompt = rms_norm(xp, final_g)

    xs = x_sample
    conv_s, gla_s = [], []
    for l in range(DEPTH):
        xs, cs, ss = run_layer(xs, l, cache_conv[l], state_gla[l], cache_mem_k[l], cache_mem_v[l])
        conv_s.append(cs)
        gla_s.append(ss)
    y_sample = rms_norm(xs, final_g)

    conv_prompt = jnp.stack(conv_p)
    conv_sample = jnp.stack(conv_s)
    gla_prompt = jnp.stack(gla_p)
    gla_sample = jnp.stack(gla_s)
    mem_k_prompt = jnp.stack(mk_p)
    mem_v_prompt = jnp.stack(mv_p)
    return (y_prompt, y_sample, conv_prompt, conv_sample, gla_prompt, gla_sample, mem_k_prompt, mem_v_prompt)


_drawn_inputs = setup_inputs


def setup_inputs(seed=0):
    import zlib

    import numpy as np

    out = dict(_drawn_inputs(seed))
    spreads = {}
    factors = {'b_dw': 3.599,
     'conv_ln_g': 5.849,
     'conv_ln_b': 7.665,
     'gla_norm_g': 6.857,
     'norm_xa_g': 8.0,
     'mem_norm_g': 2.897,
     'norm_ffn_g': 3.363,
     'final_g': 2.745}
    for name, (base, spread) in spreads.items():
        noise = np.random.default_rng([zlib.crc32(name.encode()), seed]).standard_normal(out[name].shape)
        drawn = base * np.exp(spread * noise) if base else spread * noise
        out[name] = __import__('jax').numpy.asarray(drawn.astype(out[name].dtype))
    for name, factor in factors.items():
        out[name] = (out[name] * factor).astype(out[name].dtype)
    return out
```

```python
from contextlib import ExitStack

import concourse.bass as bass
from concourse import mybir

F32 = mybir.dt.float32
F32R = mybir.dt.float32r
I8 = mybir.dt.int8
ALU = mybir.AluOpType
ACT = mybir.ActivationFunctionType
AX = mybir.AxisListType.X

P = 128
D = 1024
KT = D // P
SEQ = 1024
NS = 8
T = NS + SEQ
NB = 3
CB = T // NB
MEM = 256
EPS = 1e-6
DC = 512
CT = DC // P
CW = 31
H = 4
DK = 64
DV = 128
RANK = 16
TAU = 16.0
C = 128
NC_ = SEQ // C
HD = 256
FG = 4

T_KV = 0
T_IN = 16
N_IN = 21
T_OUT = T_IN + N_IN
T_XQ = T_OUT + KT
T_XO = T_XQ + KT
T_FF = T_XO + KT
N_T = T_FF + FG * 2 * KT
I_A, I_K, I_Q, I_V, I_R = 8, 9, 11, 13, 17
LEVELS = (1, 2, 4, 8, 16, 32, 64)
TAPS_PER_TILE = 6
N_TAPS = CT * CW

G_MEM, G_MIX, G_XA, G_FF, G_FIN = 0, 8, 16, 24, 32
P_BDW, P_LNG, P_LNB, P_GLAG, P_BAL = 40, 44, 48, 52, 53
P_WDW = 55
NPAR = P_WDW + CT * CW


def build(nc, a, o):
    names = ExitStack()
    with names:
        base = (nc.sbuf_base + 31) // 32 * 32

        def at(name, offset, shape, dt=F32):
            return nc.alloc_sbuf_tensor_at(name, shape, dt, offset=base + offset)

        def sem(name):
            return names.enter_context(nc.semaphore(name))

        SPLIT = KT * 2 * T * 4
        a_op = at("a_op", 0, [P, KT, 2, T], F32R)
        o1 = SPLIT
        w_split = at("w_split", o1, [P, 2, 2, KT, P], F32R)
        o1 += 2 * 2 * KT * P * 4
        w_raw = at("w_raw", o1, [P, 2, KT, P])
        o1 += 2 * KT * P * 4
        rstd = at("rstd", o1, [P, T])
        o1 += T * 4
        acc = at("acc", o1, [P, T])
        a_lr = at("a_lr", o1, [RANK, T])
        kv_raw = at("kv_raw", o1, [P, 4, MEM])
        o1 += T * 4
        tmp = at("tmp", o1, [P, 2, T])
        lnz = tmp[:, :, :]
        x_bd = tmp[0:NS, 0, 0:NS * DV]
        o1 += 2 * T * 4
        ident = at("ident", o1, [P, P])
        ones = at("ones", o1 + 512, [P, P])
        par = at("par", o1 + 1024, [P, NPAR])
        o2 = o1 + 1024 + (NPAR * 4 + 31) // 32 * 32
        mask = at("mask", o2, [P, len(LEVELS) + 1, P], I8)
        o2 += 1024
        walpha = at("walpha", o2, [RANK, 2 * P])
        o2 += 1024
        small = at("small", o2, [P, 160])
        o2 += 640
        o1 = (o2 + 31) // 32 * 32

        b_op = at("b_op", o1, [P, KT, 2, T], F32R)
        x_res = at("x_res", o1 + SPLIT, [P, KT, T])
        o_u, o_cs = o1, o1 + CT * (CW - 1 + SEQ) * 4
        o_y = o_cs + CT * NS * CW * 4
        o_q = o_y + CT * T * 4
        o_k = o_q + 2 * T * 4
        o_z = o_k + 2 * T * 4
        o_v = o_z + 2 * T * 4
        o_r = o_v + NC_ * DC * 4
        o_sm = o_r + H * T * 4
        conv_in = at("conv_in", o_u, [P, CT, CW - 1 + SEQ])
        conv_smp = at("conv_smp", o_cs, [P, CT, NS, CW])
        conv_y = at("conv_y", o_y, [P, CT, T])
        q_t = at("q_t", o_q, [P, 2, T])
        k_t = at("k_t", o_k, [P, 2, T])
        la = at("la", o_z, [P, 2, T])
        v_tok = at("v_tok", o_v, [P, NC_, DC])
        r_t = at("r_t", o_r, [P, H, T])
        keep = at("keep", o_sm, [P, SEQ], I8)
        v_smp = at("v_smp", o_sm + SEQ, [NS, DC])
        assert o_sm + SEQ + DC * 4 <= o1 + SPLIT + KT * T * 4
        x_in = at("x_in", o_y, [P, KT, T])
        m_op = at("m_op", o_v, [P, KT, 2, MEM], F32R)
        m_raw = at("m_raw", o_r, [P, KT, MEM])
        mvt = at("mvt", o_r + KT * MEM * 4, [P, KT, MEM])
        m_kt = at("m_kt", o_u, [P, KT, MEM])
        m_v = at("m_v", o_u + KT * MEM * 4, [P, 2, D])
        msq = at("msq", o_z, [P, KT, MEM])
        lev = at("lev", o_u, [P, 2, 2, SEQ])
        sc_t = at("sc_t", o_y, [P, NC_, H, C])
        o_t = at("o_t", o_q, [P, H, T])
        g0 = (KT // 2) * 2 * T * 4
        state = at("state", g0, [P, NC_, 2, DV])
        q_in = at("q_in", g0 + 8192, [P, 2, SEQ])
        k_in = at("k_in", g0 + 16384, [P, NC_, 2, P])
        st_smp = at("st_smp", g0 + 24576, [P, 2, NS, DV])
        k_smp = at("k_smp", o_cs - 32 + 32, [NS, 2 * P])
        ox = o1 + SPLIT
        kv = at("kv", ox, [P, 2, 2, 4, MEM], F32R)
        pt = at("pt", ox + 16384, [P, 2, 2, 512], F32R)
        ex = at("ex", ox + 24576, [P, NC_, MEM])
        qz = at("qz", o1, [P, KT, 320])
        pz = at("pz", o1 + KT * 320 * 4, [P, 2, H, 80])
        o_cache = o1 + KT * 320 * 4 + 2560
        NCS = 6
        cache = [at(f"cache{i}", o_cache + 8192 * i, [P, KT * MEM]) for i in range(NCS)]
        assert o_cache + 8192 * NCS <= o1 + SPLIT - 4096
        o_smp = at("o_smp", o1 + SPLIT - 4096, [NS, D])

        PS = [names.enter_context(nc.psum_tensor(f"ps{i}", [P, NB, 512], F32)) for i in range(2)]
        M = [names.enter_context(nc.psum_tensor(f"m{i}", [P, 512], F32)) for i in range(2)]

        par_in, m_in, x_in_s, wa_in, cs_in, st_in = (sem(n) for n in ("par_in", "m_in", "x_in_s", "wa_in", "cs_in", "st_in"))
        consts, eps_s = sem("consts"), sem("eps_s")
        w_in = [sem("w_in0"), sem("w_in1")]
        w_hi, w_lo = sem("w_hi"), sem("w_lo")
        tile_done = sem("tile_done")
        ps_free = sem("ps_free")
        op_hi, op_lo = sem("op_hi"), sem("op_lo")
        sq_s, acc_s = sem("sq_s"), sem("acc_s")
        sum_s, sumr_s, rstd_s = sem("sum_s"), sem("sumr_s"), sem("rstd_s")
        link_v, link_a, link_g = sem("link_v"), sem("link_a"), sem("link_g")
        out_s = sem("out_s")
        mv_t, mv_c = sem("mv_t"), sem("mv_c")
        gst = sem("gst")
        kvst = sem("kvst")
        sig_s, u_s, silu_s = sem("sig_s"), sem("u_s"), sem("silu_s")
        alr_s, z_s, zr_s, soft_s = sem("alr_s"), sem("z_s"), sem("zr_s"), sem("soft_s")
        vt_s, vr_s = sem("vt_s"), sem("vr_s")
        y_s, ln_s, lnr_s, mean_s, lsq_s, lacc_s, ysil_s = (sem(n) for n in ("y_s", "ln_s", "lnr_s", "mean_s", "lsq_s", "lacc_s", "ysil_s"))
        yn_s = sem("yn_s")
        lsub_s, lexp_s, lev_s, pp_s, sel_s = (sem(n) for n in ("lsub_s", "lexp_s", "lev_s", "pp_s", "sel_s"))
        qk_in_s, kx_s, qi_s, kt_s, ktr_s, kvp_s, dec_s, st_s, go_s, gor_s = (sem(n) for n in (
            "qk_in_s", "kx_s", "qi_s", "kt_s", "ktr_s", "kvp_s", "dec_s", "st_s", "go_s", "gor_s"))
        ks_s, ksr_s, vb_s, ov_s, stn_s, os_s, osr_s, sdec_s = (sem(n) for n in (
            "ks_s", "ksr_s", "vb_s", "ov_s", "stn_s", "os_s", "osr_s", "sdec_s"))
        gsq_s, gn_s, gnr_s, grs_s, gm_s = (sem(n) for n in ("gsq_s", "gn_s", "gnr_s", "grs_s", "gm_s"))
        xld, xsp = sem("xld"), sem("xsp")
        q_hi, q_lo = sem("q_hi"), sem("q_lo")
        kvr, kv_hi, kv_lo = sem("kvr"), sem("kv_hi"), sem("kv_lo")
        qk_s, nm_s, e_s, p_s, ptd, pt_hi, pt_lo, pv_s, oh_s, ol_s = (sem(n) for n in (
            "qk_s", "nm_s", "e_s", "p_s", "ptd", "pt_hi", "pt_lo", "pv_s", "oh_s", "ol_s"))
        ca = [sem(f"ca{i}") for i in range(NCS)]
        qz_s, ks2, sm_s, se_s, sp_s, spt, pz_s, cu, so_s, sor_s, sot, soh, sol = (sem(n) for n in (
            "qz_s", "ks2", "sm_s", "se_s", "sp_s", "spt", "pz_s", "cu", "so_s", "sor_s", "sot", "soh", "sol"))
        h_hi, h_lo = sem("h_hi"), sem("h_lo")
        y_out = sem("y_out")

        def cols(ap):
            return ap.rearrange("p (b c) -> p b c", b=NB)

        def pcols(i):
            return PS[i][:, :, 0:CB]

        def prompt(t2):
            return t2[:, :, NS:T]

        NR = NC_ // 2
        sc_bank = [M, [PS[0][:, 0, :], PS[0][:, 1, :]]]
        go_bank = [[PS[1][:, 0, :], PS[1][:, 1, :]], [PS[1][:, 2, :], PS[0][:, 2, :]]]
        WT = a["wt"]
        x_spill = nc.dram_tensor("x_spill", (P, KT, T), F32, kind="Internal").ap()
        block = names.enter_context(nc.Block())

        @block.sync
        def _(sp):
            sp.dma_start(m_raw[:, :, :], a["mem"]).then_inc(m_in, 16)
            sp.dma_start(par[:, :], a["par"]).then_inc(par_in, 16)

            def load_w(t, slot, wait=True):
                if wait:
                    sp.wait_ge(w_lo, t - 1)
                src = WT[t] if isinstance(t, int) else WT[bass.ds(t, 1)].rearrange("a p k n -> (a p) k n")
                sp.dma_start(w_raw[:, slot, :, :], src).then_inc(w_in[slot], 16)

            load_w(0, 0, False)
            load_w(1, 1, False)
            for t in range(2, T_XO + 2):
                load_w(t, t % 2)
                if t == 11:
                    sp.wait_ge(ps_free, KT)
                    sp.dma_start(o["mk"], m_kt[:, :, :]).then_inc(kvst, 16)
                if t == 19:
                    sp.wait_ge(mv_c, 4)
                    sp.dma_start(o["mv"], m_v[:, :, :]).then_inc(kvst, 16)
                if t == T_IN + 10:
                    sp.wait_ge(u_s, 2 * CT)
                    sp.dma_start(o["conv_p"], conv_in[:, :, SEQ:]).then_inc(kvst, 16)
                    sp.dma_start(o["conv_s"], conv_smp[:, :, :, 1:]).then_inc(kvst, 16)
                if t == T_OUT + 1:
                    sp.wait_ge(tile_done, T_OUT)
                    sp.dma_start(st_smp[:, :, :, :], a["state"]).then_inc(st_in, 16)
                    sp.wait_ge(st_s, H * NC_)
                    sp.dma_start(o["gla_p"], state[:, NC_ - 1, :, :]).then_inc(gst, 16)
                    sp.wait_ge(stn_s, 2 * H)
                    sp.dma_start(o["gla_s"], st_smp[:, :, :, :]).then_inc(gst, 16)
                    sp.wait_ge(gm_s, 3 * H - 1)
                    sp.dma_start(x_res[:, :, :], a["x"]).then_inc(xld, 16)
                if T_OUT + 3 <= t < T_XQ + 3:
                    m = t - T_OUT - 3
                    sp.wait_ge(ps_free, T_OUT + m + 1)
                    sp.dma_start(x_spill[:, m, :], x_res[:, m, :]).then_inc(xsp, 16)
                if t in (T_XQ + 3, T_XQ + 5, T_XQ + 7, T_XQ + 9):
                    h = (t - T_XQ - 3) // 2
                    if h == 0:
                        sp.wait_ge(kvst, 64)
                        sp.wait_ge(sumr_s, 7)
                    else:
                        sp.wait_ge(kv_lo, h)
                    sp.dma_start(kv_raw[:, 0:2, :], o["mk"][:, 2 * h:2 * h + 2, :]).then_inc(kvr, 16)
                    sp.dma_start(kv_raw[:, 2:4, :], o["mv"][:, :, h * HD:(h + 1) * HD]).then_inc(kvr, 16)
            sp.wait_ge(tile_done, T_XO)
            for r in range(2 * NS):
                if r >= NCS:
                    sp.wait_ge(cu, r - NCS + 1)
                src = a["cache_k"][r] if r < NS else a["cache_v"][r - NS]
                sp.dma_start(cache[r % NCS][:, :], src).then_inc(ca[r % NCS], 16)
            sp.wait_ge(pv_s, 4 * H)
            sp.wait_ge(spt, 1)
            sp.dma_start(x_res[:, :, :], x_spill[:, :, :]).then_inc(xld, 16)
            load_w(T_XO + 2, (T_XO + 2) % 2)
            first = T_XO + 3
            with sp.Fori(0, (N_T - first) // 2) as i:
                for j in range(2):
                    load_w(i * 2 + (first + j), (first + j) % 2)
            assert (N_T - first) % 2 == 1
            load_w(N_T - 1, (N_T - 1) % 2)

        @block.gpsimd
        def _(gp):
            n = 0

            def link(ins):
                nonlocal n
                n += 1
                ins.then_inc(link_g, 1)
                gp.wait_ge(link_g, n)

            link(gp.memset(ident[:, :], 0.0))
            link(gp.memset(ones[:, :], 1.0))
            link(gp.affine_select(out=ident[:, :], in_=ident[:, :], compare_op=ALU.not_equal, fill=1.0,
                                  base=0, pattern=[[-1, P]], channel_multiplier=1))
            link(gp.memset(mask[:, :, :], 1))
            diag = mask[:, len(LEVELS), :]
            link(gp.affine_select(out=diag, in_=diag, compare_op=ALU.is_equal, fill=0.0,
                                  base=0, pattern=[[-1, P]], channel_multiplier=1))
            for l, s in enumerate(LEVELS):
                m = mask[:, l, :].rearrange("p (n e s) -> p n e s", e=2, s=s)
                link(gp.memset(m[:, :, 0, :], 0))
                odd = m[:, :, 1, :]
                nb = C // (2 * s)
                link(gp.affine_select(out=odd, in_=odd, compare_op=ALU.is_ge, fill=0.0,
                                      base=0, pattern=[[-2 * s, nb], [0, s]], channel_multiplier=1))
                link(gp.affine_select(out=odd, in_=odd, compare_op=ALU.is_ge, fill=0.0,
                                      base=s - 1, pattern=[[2 * s, nb], [0, s]], channel_multiplier=-1))
            link(gp.memset(keep[:, :], 1))
            gp.memset(keep[:, :].rearrange("p (c n) -> p c n", n=C)[:, :, 0:1], 0).then_inc(consts, 1)

            def lo(t, slot):
                gp.wait_ge(w_hi, t + 1)
                gp.tensor_tensor(w_split[:, slot, 1, :, :], w_raw[:, slot, :, :],
                                 w_split[:, slot, 0, :, :].bitcast(F32), ALU.subtract).then_inc(w_lo, 1)

            lo(0, 0)
            lo(1, 1)
            with gp.Fori(1, N_T // 2) as i:
                lo(i * 2, 0)
                lo(i * 2 + 1, 1)
            lo(N_T - 1, (N_T - 1) % 2)

        @block.scalar
        def _(act):
            n = 0

            def link(ins):
                nonlocal n
                n += 1
                ins.then_inc(link_a, 1)
                act.wait_ge(link_a, n)

            def w_high(t, slot, count=None):
                if isinstance(t, int) and t >= N_T:
                    return
                act.wait_ge(w_in[slot], ((t // 2) if isinstance(t, int) else count) * 16 + 16)
                if not isinstance(t, int) or t >= 2:
                    act.wait_ge(tile_done, t - 1)
                act.activation(w_split[:, slot, 0, :, :], w_raw[:, slot, :, :], ACT.Copy).then_inc(w_hi, 1)

            def norm(k, n_sums, width=None):
                blocks = [(b * CB, CB) for b in range(NB)] if width is None else [(0, width)]
                for j, (c0, w) in enumerate(blocks):
                    act.wait_ge(sum_s, n_sums + j + 1)
                    act.activation(rstd[:, c0:c0 + w], M[j % 2][:, 0:w], ACT.Ln, bias=small[:, 128:129],
                                   scale=1.0 / D).then_inc(sumr_s, 1)
                act.wait_ge(sumr_s, n_sums + len(blocks))
                w = blocks[-1][0] + blocks[-1][1]
                act.activation(rstd[:, 0:w], rstd[:, 0:w], ACT.Exp, scale=-0.5).then_inc(rstd_s, 1)

            act.dma_start(x_in[:, :, :], a["x"]).then_inc(x_in_s, 16)
            act.dma_start(walpha[:, :], a["w_alpha"]).then_inc(wa_in, 16)
            act.dma_start(conv_smp[:, :, :, :], a["conv_cache"]).then_inc(cs_in, 16)

            w_high(0, 0)
            act.wait_ge(m_in, 16)
            act.wait_ge(par_in, 16)
            for k in range(KT):
                act.activation(m_op[:, k, 0, :], m_raw[:, k, :], ACT.Copy,
                               scale=par[:, G_MEM + k:G_MEM + k + 1]).then_inc(op_hi, 1)
            w_high(1, 1)
            act.activation(msq[:, :, :], m_raw[:, :, :], ACT.Square).then_inc(sq_s, 1)
            act.wait_ge(eps_s, 1)
            act.wait_ge(x_in_s, 16)
            for k in range(KT):
                act.activation(a_op[:, k, 0, :], x_in[:, k, :], ACT.Copy,
                               scale=par[:, G_MIX + k:G_MIX + k + 1]).then_inc(op_hi, 1)
                if k == 0:
                    norm(0, 0, MEM)
                    w_high(2, 0)
                if k == 2:
                    w_high(3, 1)
                if k == 4:
                    w_high(4, 0)
                if k == 6:
                    w_high(5, 1)
            nq = 1

            def square(src, dst_first, j, n0):
                if j == 0:
                    act.activation(acc[:, :], src, ACT.Square).then_inc(sq_s, 1)
                else:
                    if j >= 3:
                        act.wait_ge(acc_s, n0 + j - 1)
                    act.activation(tmp[:, j % 2, :], src, ACT.Square).then_inc(sq_s, 1)

            act.wait_ge(sumr_s, 1)
            for k in range(KT):
                square(x_in[:, k, :], None, k, 1)
                w_high(6 + k, k % 2)
            for t in range(14, T_IN + 2):
                w_high(t, t % 2)
            norm(1, 1)
            for i in range(N_IN):
                t = T_IN + i
                if i < 8 and i % 2 == 1:
                    act.wait_ge(ps_free, t + 1)
                    act.activation(tmp[:, 1, :], tmp[:, 1, :], ACT.Sigmoid).then_inc(sig_s, 1)
                if i >= I_R:
                    act.wait_ge(ps_free, t + 1)
                    act.activation(r_t[:, i - I_R, :], r_t[:, i - I_R, :], ACT.Silu).then_inc(silu_s, 1)
                w_high(t + 2, (t + 2) % 2)
                if i == I_K + 1:
                    act.wait_ge(zr_s, 6)
                    link(act.activation(lnz, la[:, :, :], ACT.Abs))
                    link(act.activation(lnz, lnz, ACT.Exp, scale=-1.0))
                    act.activation(lnz, lnz, ACT.Ln, bias=1.0).then_inc(soft_s, 1)

            for b in range(NB):
                act.wait_ge(ln_s, b + 1)
                act.activation(tmp[:, 0, b * CB:(b + 1) * CB], M[b % 2][:, 0:CB], ACT.Copy,
                               scale=1.0 / DC).then_inc(lnr_s, 1)
            for m in range(CT):
                act.wait_ge(mean_s, m + 1)
                if m >= 1:
                    act.wait_ge(lacc_s, m)
                dst = acc[:, :] if m == 0 else tmp[:, 1, :]
                act.activation(dst, conv_y[:, m, :], ACT.Square).then_inc(lsq_s, 1)
            for b in range(NB):
                act.wait_ge(ln_s, NB + b + 1)
                act.activation(rstd[:, b * CB:(b + 1) * CB], M[b % 2][:, 0:CB], ACT.Ln,
                               bias=small[:, 128:129], scale=1.0 / DC).then_inc(lnr_s, 1)
            act.wait_ge(lnr_s, 2 * NB)
            act.activation(rstd[:, :], rstd[:, :], ACT.Exp, scale=-0.5).then_inc(lnr_s, 1)
            act.wait_ge(tile_done, T_OUT)
            for m in range(CT):
                act.wait_ge(yn_s, m + 1)
                act.activation(conv_y[:, m, :], conv_y[:, m, :], ACT.Silu, bias=par[:, P_LNB + m:P_LNB + m + 1],
                               scale=par[:, P_LNG + m:P_LNG + m + 1]).then_inc(ysil_s, 1)
            for m in range(CT):
                act.wait_ge(ysil_s, m + 1)
                act.activation(a_op[:, m, 0, :], conv_y[:, m, :], ACT.Copy).then_inc(op_hi, 1)

            for l in range(len(LEVELS)):
                act.wait_ge(lsub_s, l + 1)
                act.activation(lev[:, l % 2, :, :], lev[:, l % 2, :, :], ACT.Exp, scale=1.0 / TAU).then_inc(lexp_s, 1)
            act.wait_ge(qk_in_s, 1)
            act.activation(q_in[:, :, :], prompt(la), ACT.Exp, scale=1.0 / TAU).then_inc(kx_s, 1)
            act.activation(lev[:, 1, :, :], lev[:, 1, :, :], ACT.Exp, scale=1.0 / TAU).then_inc(kx_s, 1)
            last = prompt(la).rearrange("p a (c n) -> p a c n", n=C)[:, :, :, C - 1]
            act.activation(small[:, 0:16].rearrange("p (a c) -> p a c", a=2), last, ACT.Exp,
                           scale=1.0 / TAU).then_inc(dec_s, 1)
            act.activation(small[:, 16:32].rearrange("p (a s) -> p a s", a=2), la[:, :, 0:NS], ACT.Exp,
                           scale=1.0 / TAU).then_inc(dec_s, 1)
            for h in range(H):
                act.wait_ge(gor_s, NC_)
                act.wait_ge(osr_s, 2)
                if h >= 1:
                    act.wait_ge(gn_s, NB * h)
                act.activation(tmp[:, 0, :], o_t[:, h, :], ACT.Square).then_inc(gsq_s, 1)
                if h >= 1:
                    act.wait_ge(gm_s, 3 * h)
                for b in range(NB):
                    act.wait_ge(gn_s, NB * h + b + 1)
                    act.activation(tmp[:, 1, b * CB:(b + 1) * CB], M[b % 2][:, 0:CB], ACT.Ln,
                                   bias=small[:, 128:129], scale=1.0 / DV).then_inc(gnr_s, 1)
                act.wait_ge(gnr_s, NB * (h + 1))
                act.activation(tmp[:, 1, :], tmp[:, 1, :], ACT.Exp, scale=-0.5).then_inc(grs_s, 1)
                act.wait_ge(gm_s, 3 * h + 2)
                if h == 0:
                    act.wait_ge(gst, 32)
                act.activation(a_op[:, CT + h, 0, :], o_t[:, h, :], ACT.Copy).then_inc(op_hi, 1)

            def residual_tile(t, m, gain, n_op, n_sq):
                act.wait_ge(ps_free, t + 1)
                if gain is not None:
                    act.activation(b_op[:, m, 0, :], x_res[:, m, :], ACT.Copy,
                                   scale=par[:, gain + m:gain + m + 1]).then_inc(op_hi, 1)
                square(x_res[:, m, :], None, m, n_sq)
                w_high(t + 2, (t + 2) % 2)

            for m in range(KT):
                residual_tile(T_OUT + m, m, G_XA, 24, 9)
            norm(2, 4)

            def kv_high(h):
                act.wait_ge(kvr, 32 * (h + 1))
                if h >= 2:
                    act.wait_ge(pv_s, 4 * (h - 1))
                act.activation(kv[:, h % 2, 0, :, :], kv_raw[:, :, :], ACT.Copy).then_inc(kv_hi, 1)

            def q_tiles(h):
                for j in range(2):
                    t = T_XQ + 2 * h + j
                    act.wait_ge(ps_free, t + 1)
                    act.activation(a_op[:, 2 * h + j, 0, :], tmp[:, j, :], ACT.Copy).then_inc(q_hi, 1)
                    w_high(t + 2, (t + 2) % 2)

            q_tiles(0)
            act.wait_ge(xsp, 16 * KT)
            kv_high(0)
            for h in range(H):
                for c in range(NC_):
                    if h >= 1 and c == 0:
                        act.wait_ge(ptd, 2 * h)
                    act.wait_ge(nm_s, NC_ * h + c + 1)
                    act.activation(ex[:, c, :], M[c % 2][:, 0:MEM], ACT.Exp, bias=small[:, 32 + c:33 + c],
                                   scale=HD ** -0.5, accum_out=small[:, 40 + c:41 + c]).then_inc(e_s, 1)
                if h + 1 < H:
                    kv_high(h + 1)
                    q_tiles(h + 1)
                for u in range(2):
                    act.wait_ge(ptd, 2 * h + u + 1)
                    if 2 * h + u >= 1:
                        act.wait_ge(pv_s, 2 * (2 * h + u))
                    act.activation(pt[:, :, 0, :], PS[u][:, 0:2, :], ACT.Copy).then_inc(pt_hi, 1)
                for u in range(2):
                    for d in range(2):
                        act.wait_ge(pv_s, 4 * h + 2 * u + d + 1)
                        src = PS[u][:, 2, :] if d == 0 else M[u][:, :]
                        act.activation(a_op[:, 2 * h + d, 0, NS + 512 * u:NS + 512 * (u + 1)], src,
                                       ACT.Copy).then_inc(oh_s, 1)
            act.wait_ge(sm_s, 1)
            act.activation(ex[0:32, 0, :], M[0][0:32, 0:MEM], ACT.Exp, bias=small[0:32, 32:33],
                           scale=HD ** -0.5, accum_out=small[0:32, 40:41]).then_inc(se_s, 1)
            act.wait_ge(sot, 1)
            act.activation(a_op[:, :, 0, 0:NS], M[0][:, 0:KT * NS].rearrange("p (k s) -> p k s", s=NS),
                           ACT.Copy).then_inc(soh, 1)

            for m in range(KT):
                residual_tile(T_XO + m, m, G_FF, 32, 17)
            norm(3, 7)

            def up(t, j, m, count):
                act.wait_ge(ps_free, t + 1)
                act.activation(tmp[:, j, :], tmp[:, j, :], ACT.Square).then_inc(link_a, 1)
                act.wait_ge(link_a, n_up0 + count + 1)
                dst = a_op[:, bass.ds(m, 1), 0, :].rearrange("p a n -> p (a n)")
                act.activation(dst, tmp[:, j, :], ACT.Copy).then_inc(h_hi, 1)

            n_up0 = n
            half = T_FF // 2
            with act.Fori(0, FG - 1) as g:
                with act.Fori(0, KT // 2) as i:
                    for j in range(2):
                        t = g * 16 + i * 2 + (T_FF + j)
                        up(t, j, i * 2 + j, g * 8 + i * 2 + j)
                        w_high(t + 2, (T_FF + j) % 2, g * 8 + i + ((T_FF + j) // 2 + 1))
                with act.Fori(0, KT // 2) as i:
                    for j in range(2):
                        t = g * 16 + i * 2 + (T_FF + KT + j)
                        w_high(t + 2, (T_FF + j) % 2, g * 8 + i + ((T_FF + KT + j) // 2 + 1))
            g = FG - 1
            with act.Fori(0, KT // 2) as i:
                for j in range(2):
                    t = i * 2 + (T_FF + 16 * g + j)
                    up(t, j, i * 2 + j, i * 2 + (g * 8 + j))
                    w_high(t + 2, (T_FF + j) % 2, i + ((T_FF + 16 * g + j) // 2 + 1))
            for m in range(KT):
                residual_tile(T_FF + 16 * g + KT + m, m, None, 0, 25)
            norm(4, 10)
            for m in range(KT):
                act.wait_ge(y_out, m + 1)
                act.dma_start(o["y"][:, m, :], x_res[:, m, :]).then_inc(out_s, 16)
            act.wait_ge(out_s, 16 * KT)

        @block.tensor
        def _(pe):
            def tile_product(t, slot, src, blocks, k_wait):
                pe.wait_ge(w_lo, t + 1)
                if not isinstance(t, int) or t >= 2:
                    pe.wait_ge(ps_free, t - 1)
                ps = PS[slot]
                for k in range(KT):
                    k_wait(k)
                    for j, (wp, xp) in enumerate(((0, 0), (0, 1), (1, 0))):
                        for b, (c0, w) in enumerate(blocks):
                            last = pe.matmul(ps[:, b, 0:w], w_split[:, slot, wp, k, :], src[:, k, xp, c0:c0 + w],
                                             start=(k == 0 and j == 0), stop=(k == KT - 1 and j == 2))
                last.then_inc(tile_done, 1)

            ALL = [(b * CB, CB) for b in range(NB)]

            def wait_lo(n0):
                return lambda k: pe.wait_ge(op_lo, n0 + k + 1)

            def no_wait(k):
                return None

            def sums(need, n_sums, width=None):
                pe.wait_ge(acc_s, need)
                for j, (c0, w) in enumerate(ALL if width is None else [(0, width)]):
                    if j >= 2:
                        pe.wait_ge(sumr_s, n_sums + j - 1)
                    pe.matmul(M[j % 2][:, 0:w], ones[:, :], acc[:, c0:c0 + w], start=True, stop=True).then_inc(sum_s, 1)

            pe.wait_ge(consts, 1)
            for t in range(16):
                tile_product(t, t % 2, m_op, [(0, MEM)], wait_lo(0) if t == 0 else no_wait)
                if t == 0:
                    sums(1, 0, MEM)
            for g in range(4):
                pe.wait_ge(ps_free, 9 + 2 * g + 1)
                if g >= 2:
                    pe.wait_ge(mv_c, g - 1)
                for j in range(2):
                    for mt in range(2):
                        last = pe.transpose(M[g % 2][:, (2 * mt + j) * P:(2 * mt + j + 1) * P],
                                            mvt[:, 2 * g + j, mt * P:(mt + 1) * P], ident[:, :])
                last.then_inc(mv_t, 1)
            def v_turn(m):
                for g in range(2):
                    if m >= 1:
                        pe.wait_ge(vr_s, 3 * m)
                    for j in range(4):
                        c = 4 * g + j
                        last = pe.transpose(M[g][:, j * P:(j + 1) * P],
                                            tmp[:, (I_V + m) % 2, NS + C * c:NS + C * (c + 1)], ident[:, :])
                    last.then_inc(vt_s, 1)
                pe.wait_ge(vr_s, 3 * m + 1)
                pe.transpose(M[0][0:NS, 0:P], tmp[:, (I_V + m) % 2, 0:NS], ident[:, :]).then_inc(vt_s, 1)

            for i in range(N_IN):
                t = T_IN + i
                tile_product(t, t % 2, a_op, ALL, wait_lo(8) if i == 0 else no_wait)
                if i == 0:
                    pe.wait_ge(mv_c, 4)
                    sums(9, 1)
                if i == I_K:
                    pe.wait_ge(alr_s, 1)
                    pe.wait_ge(wa_in, 16)
                    pe.wait_ge(sumr_s, 4)
                    for j in range(2 * NB):
                        pair, b = divmod(j, NB)
                        if j >= 2:
                            pe.wait_ge(zr_s, j - 1)
                        pe.matmul(M[j % 2][:, 0:CB], walpha[:, pair * P:(pair + 1) * P],
                                  a_lr[:, b * CB:(b + 1) * CB], start=True, stop=True).then_inc(z_s, 1)
                if I_V < i <= I_V + 4:
                    m = i - I_V - 1
                    pe.wait_ge(ps_free, T_IN + I_V + m + 1)
                    if m == 0:
                        pe.wait_ge(zr_s, 6)
                    v_turn(m)

            pe.wait_ge(vr_s, 12)
            pe.wait_ge(y_s, 1)
            for j in range(NB):
                if j >= 2:
                    pe.wait_ge(lnr_s, j - 1)
                pe.matmul(M[j % 2][:, 0:CB], ones[:, :], acc[:, j * CB:(j + 1) * CB], start=True, stop=True).then_inc(ln_s, 1)
            pe.wait_ge(lacc_s, CT)
            pe.wait_ge(lnr_s, NB)
            for j in range(NB):
                if j >= 2:
                    pe.wait_ge(lnr_s, NB + j - 1)
                pe.matmul(M[j % 2][:, 0:CB], ones[:, :], acc[:, j * CB:(j + 1) * CB], start=True, stop=True).then_inc(ln_s, 1)
            pe.wait_ge(lnr_s, 2 * NB)

            nl = len(LEVELS)
            for l in range(nl + 1):
                if l < nl:
                    pe.wait_ge(lev_s, 2 * (l + 1))
                for r in range(NR):
                    if NR * l + r >= 2:
                        pe.wait_ge(sel_s, 2 * (NR * l + r - 1))
                    for j in range(4):
                        c, pair = 2 * r + j // 2, j % 2
                        for par_ in range(2):
                            p0 = DK * par_
                            if l < nl:
                                kk = lev[p0:p0 + DK, l % 2, pair, C * c:C * (c + 1)]
                                qq = kk
                            else:
                                kk = k_t[p0:p0 + DK, pair, NS + C * c:NS + C * (c + 1)]
                                qq = q_t[p0:p0 + DK, pair, NS + C * c:NS + C * (c + 1)]
                            last = pe.matmul(sc_bank[r % 2][par_][:, j * C:(j + 1) * C], kk, qq, start=True, stop=True)
                    last.then_inc(pp_s, 1)
            pe.wait_ge(qi_s, 2)
            for g in range(4):
                if g == 0:
                    pe.wait_ge(sel_s, 2 * NR * (nl + 1))
                if g >= 2:
                    pe.wait_ge(ktr_s, g - 1)
                for j in range(4):
                    c, pair = 2 * g + j // 2, j % 2
                    last = pe.transpose(M[g % 2][:, j * P:(j + 1) * P], lev[:, 1, pair, C * c:C * (c + 1)], ident[:, :])
                last.then_inc(kt_s, 1)
            pe.wait_ge(ktr_s, 4)
            for pair in range(2):
                last = pe.transpose(M[0][0:NS, pair * P:(pair + 1) * P], k_t[:, pair, 0:NS], ident[:, :])
            last.then_inc(ks_s, 1)
            for c in range(NC_):
                if c >= 2:
                    pe.wait_ge(st_s, 4 * (c - 1))
                for pair in range(2):
                    last = pe.matmul(PS[0][:, c % 2, pair * 256:(pair + 1) * 256], k_in[:, c, pair, :],
                                     v_tok[:, c, pair * 256:(pair + 1) * 256], start=True, stop=True)
                last.then_inc(kvp_s, 1)
            for r in range(NR):
                pe.wait_ge(st_s, 4 * (2 * r + 1))
                if r >= 2:
                    pe.wait_ge(gor_s, 2 * (r - 1))
                for j in range(4):
                    c, pair = 2 * r + j // 2, j % 2
                    for par_ in range(2):
                        h, p0 = 2 * pair + par_, DK * par_
                        dst = go_bank[r % 2][par_][:, j * C:(j + 1) * C]
                        last = pe.matmul(dst, v_tok[:, c, h * DV:(h + 1) * DV], sc_t[:, c, h, :], start=True, stop=(c == 0))
                        if c >= 1:
                            last = pe.matmul(dst, state[p0:p0 + DK, c - 1, pair, :],
                                             q_in[p0:p0 + DK, pair, C * c:C * (c + 1)], start=False, stop=True)
                last.then_inc(go_s, 1)
            for h in range(H):
                pe.wait_ge(vb_s, h + 1)
                for g in range(2):
                    if 2 * h + g >= 1:
                        pe.wait_ge(stn_s, 2 * h + g)
                    if h == 0 and g == 0:
                        pe.wait_ge(ksr_s, 1)
                    p0 = DK * (h % 2)
                    pe.matmul(M[1][p0:p0 + DK, :], k_smp[:, h * DK:(h + 1) * DK],
                              x_bd[:, g * 512:(g + 1) * 512], start=True, stop=True).then_inc(ov_s, 1)
            pe.wait_ge(stn_s, 8)
            for h in range(H):
                p0, pair = DK * (h % 2), h // 2
                for s in range(NS):
                    last = pe.matmul(M[h % 2][:, pair * NS + s:pair * NS + s + 1], st_smp[p0:p0 + DK, pair, s, :],
                                     small[p0:p0 + DK, 48 + pair * NS + s:49 + pair * NS + s], start=True, stop=True)
            last.then_inc(os_s, 1)
            pe.wait_ge(osr_s, 2)
            for h in range(H):
                pe.wait_ge(gsq_s, h + 1)
                for j in range(NB):
                    r = NB * h + j
                    if r >= 2:
                        pe.wait_ge(gnr_s, r - 1 if j >= 2 else NB * h)
                    pe.matmul(M[j % 2][:, 0:CB], ones[:, :], tmp[:, 0, j * CB:(j + 1) * CB], start=True, stop=True).then_inc(gn_s, 1)

            def wait_mix(k):
                pe.wait_ge(op_lo, 17 + k)

            pe.wait_ge(gor_s, NC_)
            for m in range(KT):
                t = T_OUT + m
                tile_product(t, t % 2, a_op, ALL, wait_mix if m == 0 else no_wait)

            def q_tiles(h):
                for j in range(2):
                    t = T_XQ + 2 * h + j
                    tile_product(t, t % 2, b_op, ALL, wait_lo(24) if t == T_XQ else no_wait)
                    if t == T_XQ:
                        sums(17, 4)

            q_tiles(0)
            for h in range(H):
                pe.wait_ge(kv_lo, h + 1)
                pe.wait_ge(q_lo, 2 * h + 2)
                if h == 0:
                    pe.wait_ge(sumr_s, 7)
                for c in range(NC_):
                    if c >= 2:
                        pe.wait_ge(e_s, NC_ * h + c - 1)
                    elif h >= 1:
                        pe.wait_ge(ol_s, 4 * h)
                    c0 = NS + C * c
                    for k in range(2):
                        for j, (qp, kp) in enumerate(((0, 0), (0, 1), (1, 0))):
                            last = pe.matmul(M[c % 2][:, 0:MEM], a_op[:, 2 * h + k, qp, c0:c0 + C], kv[:, h % 2, kp, k, :],
                                             start=(k == 0 and j == 0), stop=(k == 1 and j == 2))
                    last.then_inc(qk_s, 1)
                if h + 1 < H:
                    q_tiles(h + 1)
                t_last = T_XQ + 2 * min(h + 1, H - 1) + 1
                pe.wait_ge(ps_free, t_last + 1)
                for u in range(2):
                    pe.wait_ge(p_s, NC_ * h + 4 * (u + 1))
                    for mt in range(2):
                        for j in range(4):
                            last = pe.transpose(PS[u][:, mt, j * C:(j + 1) * C],
                                                ex[:, 4 * u + j, mt * P:(mt + 1) * P], ident[:, :])
                    last.then_inc(ptd, 1)
                for u in range(2):
                    pe.wait_ge(pt_lo, 2 * h + u + 1)
                    for d in range(2):
                        dst = PS[u][:, 2, :] if d == 0 else M[u][:, :]
                        for mt in range(2):
                            for j, (vp, pp) in enumerate(((0, 0), (0, 1), (1, 0))):
                                last = pe.matmul(dst, kv[:, h % 2, vp, 2 + mt, d * P:(d + 1) * P], pt[:, mt, pp, :],
                                                 start=(mt == 0 and j == 0), stop=(mt == 1 and j == 2))
                        last.then_inc(pv_s, 1)
            pe.wait_ge(qz_s, 1)
            pe.wait_ge(ol_s, 16)
            for s in range(NS):
                pe.wait_ge(ca[s % NCS], 16 * (s // NCS + 1))
                for k in range(KT):
                    r = H * s + k // 2
                    p0 = 32 + 32 * s - r
                    last = pe.matmul(M[0][0:32, 0:MEM], qz[:, k, p0:p0 + 32], cache[s % NCS][:, k * MEM:(k + 1) * MEM],
                                     start=(s == 0 and k == 0), stop=(s == NS - 1 and k == KT - 1))
                last.then_inc(cu, 1)
            pe.wait_ge(sp_s, 1)
            for mt in range(2):
                last = pe.transpose(M[1][:, mt * 32:(mt + 1) * 32], ex[0:32, 0, mt * P:(mt + 1) * P], ident[0:32, 0:32])
            last.then_inc(spt, 1)
            pe.wait_ge(pz_s, 3)
            for s in range(NS):
                r = NS + s
                pe.wait_ge(ca[r % NCS], 16 * (r // NCS + 1))
                for h in range(H):
                    dst = PS[0][0:NS, h, 0:HD] if h < 3 else PS[1][0:NS, 0, 0:HD]
                    for mt in range(2):
                        last = pe.matmul(dst, pz[:, mt, h, 8 + 7 * s:16 + 7 * s],
                                         cache[r % NCS][:, mt * D + h * HD:mt * D + (h + 1) * HD],
                                         start=(s == 0 and mt == 0), stop=(s == NS - 1 and mt == 1))
                last.then_inc(cu, 1)
            pe.wait_ge(sor_s, 2)
            for k in range(KT):
                last = pe.transpose(M[0][:, k * NS:(k + 1) * NS], o_smp[:, k * P:(k + 1) * P], ident[0:NS, 0:NS])
            last.then_inc(sot, 1)

            pe.wait_ge(sol, 1)
            for m in range(KT):
                t = T_XO + m
                tile_product(t, t % 2, a_op, ALL, no_wait)

            def last_two(sem_, n0):
                def wait(k):
                    if k == 0:
                        pe.wait_ge(sem_, n0 + (KT - 1))
                    if k == KT - 1:
                        pe.wait_ge(sem_, n0 + KT)
                return wait

            def ffn_group(g, first=False, rest=0):
                with pe.Fori(1 if first else 0, KT // 2) as i:
                    for j in range(2):
                        tile_product(g * 16 + i * 2 + (T_FF + j), (T_FF + j) % 2, b_op, ALL, no_wait)
                with pe.Fori(0, KT // 2) as i:
                    for j in range(2):
                        tile_product(g * 16 + i * 2 + (T_FF + KT + j), (T_FF + j) % 2, a_op, ALL,
                                     last_two(h_lo, g * 8))

            tile_product(T_FF, T_FF % 2, b_op, ALL, wait_lo(32))
            sums(25, 7)
            tile_product(T_FF + 1, (T_FF + 1) % 2, b_op, ALL, no_wait)
            ffn_group(0, first=True)
            with pe.Fori(1, FG) as g:
                ffn_group(g)
            sums(33, 10)

        @block.vector
        def _(dve):
            n = 0

            def link(ins):
                nonlocal n
                n += 1
                ins.then_inc(link_v, 1)
                dve.wait_ge(link_v, n)

            dve.memset(small[:, 128:129], EPS).then_inc(eps_s, 1)

            def low(dst, src, gain, hi, sem_, need):
                dve.wait_ge(sem_, need)
                if gain is None:
                    return dve.tensor_tensor(dst, src, hi.bitcast(F32), ALU.subtract)
                return dve.scalar_tensor_tensor(out=dst, in0=src, scalar=gain, in1=hi.bitcast(F32),
                                                op0=ALU.mult, op1=ALU.subtract)

            dve.wait_ge(m_in, 16)
            for k in range(KT):
                low(m_op[:, k, 1, :], m_raw[:, k, :], par[:, G_MEM + k:G_MEM + k + 1], m_op[:, k, 0, :],
                    op_hi, k + 1).then_inc(op_lo, 1)
            dve.wait_ge(sq_s, 1)
            dve.tensor_reduce(acc[:, 0:MEM], msq[:, :, :].rearrange("p k n -> p n k"), AX, ALU.add).then_inc(acc_s, 1)

            def m_evac(t):
                dve.wait_ge(tile_done, t + 1)
                if t == 0:
                    dve.wait_ge(rstd_s, 1)
                dst = m_kt[:, t, :] if t < KT else mvt[:, t - KT, :]
                dve.tensor_tensor(dst, PS[t % 2][:, 0, 0:MEM], rstd[:, 0:MEM], ALU.mult).then_inc(ps_free, 1)

            for t in range(16):
                m_evac(t)
                if t % 2 == 1:
                    k = t // 2
                    low(a_op[:, k, 1, :], x_in[:, k, :], par[:, G_MIX + k:G_MIX + k + 1], a_op[:, k, 0, :],
                        op_hi, 8 + k + 1).then_inc(op_lo, 1)
                if t >= 6 and t - 6 < KT:
                    k = t - 6
                    dve.wait_ge(sq_s, 1 + k + 1)
                    if k == 0:
                        dve.engine_nop().then_inc(acc_s, 1)
                    else:
                        dve.wait_ge(acc_s, 1 + k)
                        dve.tensor_tensor(acc[:, :], acc[:, :], tmp[:, k % 2, :], ALU.add).then_inc(acc_s, 1)
            for g in range(4):
                dve.wait_ge(mv_t, g + 1)
                dve.tensor_copy(m_v[:, :, 2 * g * P:(2 * g + 2) * P],
                                M[g % 2][:, :].rearrange("p (a n) -> p a n", a=2)).then_inc(mv_c, 1)
            dve.wait_ge(kvst, 32)
            link(dve.memset(conv_in[:, :, 0:CW - 1], 0.0))

            def taps(n0, n1):
                for j in range(n0, min(n1, N_TAPS)):
                    m, w = divmod(j, CW)
                    dst = conv_y[:, m, NS:T]
                    src = conv_in[:, m, w:w + SEQ]
                    tap = par[:, P_WDW + m * CW + w:P_WDW + m * CW + w + 1]
                    if w == 0:
                        link(dve.tensor_scalar(dst, src, tap, par[:, P_BDW + m:P_BDW + m + 1], ALU.mult, ALU.add))
                    else:
                        link(dve.scalar_tensor_tensor(out=dst, in0=src, scalar=tap, in1=dst, op0=ALU.mult, op1=ALU.add))

            def v_evac(m):
                for g in range(2):
                    dve.wait_ge(vt_s, 3 * m + g + 1)
                    dve.tensor_copy(v_tok[:, 4 * g:4 * g + 4, m * P:(m + 1) * P],
                                    M[g][:, :].rearrange("p (c n) -> p c n", c=4)).then_inc(vr_s, 1)
                dve.wait_ge(vt_s, 3 * m + 3)
                dve.tensor_copy(v_smp[:, m * P:(m + 1) * P], M[0][0:NS, 0:P]).then_inc(vr_s, 1)

            for i in range(N_IN):
                t = T_IN + i
                dve.wait_ge(tile_done, t + 1)
                if i == 0:
                    dve.wait_ge(rstd_s, 2)
                ps = pcols(t % 2)
                if i < 8:
                    m, gate = divmod(i, 2)
                    dve.tensor_tensor(cols(tmp[:, gate, :]), ps, cols(rstd[:, :]), ALU.mult).then_inc(ps_free, 1)
                    if gate:
                        dve.wait_ge(sig_s, m + 1)
                        if m == 0:
                            dve.wait_ge(cs_in, 16)
                        dve.tensor_tensor(conv_in[:, m, CW - 1:], tmp[:, 0, NS:T], tmp[:, 1, NS:T], ALU.mult).then_inc(u_s, 1)
                        dve.tensor_tensor(conv_smp[:, m, :, CW - 1], tmp[:, 0, 0:NS], tmp[:, 1, 0:NS], ALU.mult).then_inc(u_s, 1)
                        dve.wait_ge(u_s, 2 * m + 2)
                elif i == I_A:
                    dve.tensor_tensor(cols(a_lr[:, :]), PS[t % 2][0:RANK, :, 0:CB], cols(rstd[0:RANK, :]),
                                      ALU.mult).then_inc(ps_free, 1)
                elif i < I_Q:
                    dve.tensor_tensor(cols(k_t[:, i - I_K, :]), ps, cols(rstd[:, :]), ALU.mult).then_inc(ps_free, 1)
                elif i < I_V:
                    dve.scalar_tensor_tensor(out=cols(q_t[:, i - I_Q, :]), in0=ps, scalar=DK ** -0.5, in1=cols(rstd[:, :]),
                                             op0=ALU.mult, op1=ALU.mult).then_inc(ps_free, 1)
                elif i < I_R:
                    dve.tensor_tensor(cols(tmp[:, i % 2, :]), ps, cols(rstd[:, :]), ALU.mult).then_inc(ps_free, 1)
                else:
                    dve.tensor_tensor(cols(r_t[:, i - I_R, :]), ps, cols(rstd[:, :]), ALU.mult).then_inc(ps_free, 1)
                if i == I_A:
                    dve.wait_ge(ps_free, t + 1)
                    dve.engine_nop().then_inc(alr_s, 1)
                if i == I_K:
                    for j in range(2 * NB):
                        pair, b = divmod(j, NB)
                        dve.wait_ge(z_s, j + 1)
                        dve.tensor_scalar(la[:, pair, b * CB:(b + 1) * CB], M[j % 2][:, 0:CB],
                                          par[:, P_BAL + pair:P_BAL + pair + 1], None, ALU.add).then_inc(zr_s, 1)
                if i == I_Q:
                    dve.wait_ge(soft_s, 1)
                    link(dve.scalar_tensor_tensor(out=la[:, :, :], in0=la[:, :, :], scalar=0.0, in1=lnz,
                                                  op0=ALU.min, op1=ALU.subtract))
                    for pair in range(2):
                        z = la[:, pair, NS:T]
                        link(dve.tensor_tensor_scan(z, keep[:, :], z, 0.0, ALU.mult, ALU.add))
                if I_V < i <= I_V + 4:
                    v_evac(i - I_V - 1)
                if i >= 1:
                    taps(TAPS_PER_TILE * (i - 1), TAPS_PER_TILE * i)
            taps(TAPS_PER_TILE * (N_IN - 1), N_TAPS)

            for m in range(CT):
                wd = par[:, P_WDW + m * CW:P_WDW + (m + 1) * CW].unsqueeze(1).broadcast_to([P, NS, CW])
                prod = tmp[:, 0, 0:NS * CW].rearrange("p (s w) -> p s w", s=NS)
                link(dve.tensor_tensor(prod, conv_smp[:, m, :, :], wd, ALU.mult))
                link(dve.tensor_reduce(conv_y[:, m, 0:NS], prod, AX, ALU.add))
                link(dve.tensor_scalar(conv_y[:, m, 0:NS], conv_y[:, m, 0:NS], par[:, P_BDW + m:P_BDW + m + 1], None, ALU.add))
            link(dve.tensor_tensor(acc[:, :], conv_y[:, 0, :], conv_y[:, 1, :], ALU.add))
            link(dve.tensor_tensor(acc[:, :], acc[:, :], conv_y[:, 2, :], ALU.add))
            dve.tensor_tensor(acc[:, :], acc[:, :], conv_y[:, 3, :], ALU.add).then_inc(y_s, 1)
            dve.wait_ge(lnr_s, NB)
            for m in range(CT):
                dve.tensor_tensor(conv_y[:, m, :], conv_y[:, m, :], tmp[:, 0, :], ALU.subtract).then_inc(mean_s, 1)
            for m in range(CT):
                dve.wait_ge(lsq_s, m + 1)
                if m == 0:
                    dve.engine_nop().then_inc(lacc_s, 1)
                else:
                    dve.wait_ge(lacc_s, m)
                    dve.tensor_tensor(acc[:, :], acc[:, :], tmp[:, 1, :], ALU.add).then_inc(lacc_s, 1)
            dve.wait_ge(lnr_s, 2 * NB + 1)
            for m in range(CT):
                dve.tensor_tensor(conv_y[:, m, :], conv_y[:, m, :], rstd[:, :], ALU.mult).then_inc(yn_s, 1)
            dve.wait_ge(tile_done, T_OUT)
            for m in range(CT):
                low(a_op[:, m, 1, :], conv_y[:, m, :], None, a_op[:, m, 0, :], op_hi, 16 + m + 1).then_inc(op_lo, 1)

            dve.wait_ge(kvst, 48 + 16)
            dve.wait_ge(op_lo, 20)
            link(dve.memset(sc_t[:, :, :, :], 0.0))

            def halves(ap, s):
                v = ap.rearrange("p a (n e s) -> p a n e s", e=2, s=s)
                return v[:, :, :, 0, :], v[:, :, :, 1, :]

            nl = len(LEVELS)

            def level_sub(l):
                s = LEVELS[l]
                be, bo = halves(prompt(la), s)
                ee, eo = halves(lev[:, l % 2, :, :], s)
                end = be[:, :, :, s - 1:s].broadcast_to([P, 2, SEQ // (2 * s), s])
                if l >= 2:
                    dve.wait_ge(pp_s, NR * (l - 1))
                link(dve.tensor_tensor(eo, bo, end, ALU.subtract))
                dve.tensor_tensor(ee, end, be, ALU.subtract).then_inc(lsub_s, 1)

            def level_mul(l):
                s = LEVELS[l]
                dve.wait_ge(lexp_s, l + 1)
                ke, _ = halves(prompt(k_t), s)
                _, qo = halves(prompt(q_t), s)
                ee, eo = halves(lev[:, l % 2, :, :], s)
                dve.tensor_tensor(eo, eo, qo, ALU.mult).then_inc(lev_s, 1)
                dve.tensor_tensor(ee, ee, ke, ALU.mult).then_inc(lev_s, 1)

            level_sub(0)
            level_mul(0)
            for l in range(nl + 1):
                if l + 1 < nl:
                    level_sub(l + 1)
                for r in range(NR):
                    dve.wait_ge(pp_s, NR * l + r + 1)
                    mk = mask[:, l, :].unsqueeze(1).unsqueeze(1).broadcast_to([P, 2, 2, C])
                    for par_ in range(2):
                        dst = sc_t[:, 2 * r:2 * r + 2, :, :].rearrange("p c (a b) n -> p c a b n", b=2)[:, :, :, par_, :]
                        dve.copy_predicated(dst, mk, sc_bank[r % 2][par_][:, :].rearrange(
                            "p (c a n) -> p c a n", c=2, a=2)).then_inc(sel_s, 1)
                    if r == 0 and l + 1 < nl:
                        level_mul(l + 1)

            dve.wait_ge(sel_s, 2 * NR * (nl + 1))
            b4 = prompt(la).rearrange("p a (c n) -> p a c n", n=C)
            endb = b4[:, :, :, C - 1:C].broadcast_to([P, 2, NC_, C])
            dve.tensor_tensor(lev[:, 1, :, :].rearrange("p a (c n) -> p a c n", n=C), endb, b4, ALU.subtract).then_inc(qk_in_s, 1)
            link(dve.tensor_copy(small[:, 48:64].rearrange("p (a s) -> p a s", a=2), q_t[:, :, 0:NS]))
            dve.wait_ge(kx_s, 1)
            dve.tensor_tensor(q_in[:, :, :], q_in[:, :, :], prompt(q_t), ALU.mult).then_inc(qi_s, 1)
            dve.wait_ge(kx_s, 2)
            dve.tensor_tensor(lev[:, 1, :, :], lev[:, 1, :, :], prompt(k_t), ALU.mult).then_inc(qi_s, 1)
            for g in range(4):
                dve.wait_ge(kt_s, g + 1)
                dve.tensor_copy(k_in[:, 2 * g:2 * g + 2, :, :],
                                M[g % 2][:, :].rearrange("p (c a n) -> p c a n", c=2, a=2)).then_inc(ktr_s, 1)
            dve.wait_ge(ks_s, 1)
            dve.tensor_copy(k_smp[:, :], M[0][0:NS, 0:2 * P]).then_inc(ksr_s, 1)
            dve.wait_ge(st_in, 16)
            dve.wait_ge(dec_s, 2)
            dec = small[:, 16:32].unsqueeze(2).broadcast_to([P, 2 * NS, DV])
            ss = st_smp[:, :, :, :].rearrange("p a s v -> p (a s) v")
            link(dve.tensor_tensor(ss, ss, dec, ALU.mult))

            def out_evac(r):
                dve.wait_ge(go_s, r + 1)
                for par_ in range(2):
                    dst = o_t[:, :, NS + 2 * C * r:NS + 2 * C * (r + 1)].rearrange(
                        "p (a b) (c n) -> p a b c n", b=2, c=2)[:, :, par_, :, :]
                    dve.tensor_copy(dst, go_bank[r % 2][par_][:, :].rearrange(
                        "p (c a n) -> p a c n", c=2, a=2)).then_inc(gor_s, 1)

            for c in range(NC_):
                dve.wait_ge(kvp_s, c + 1)
                for h in range(H):
                    p0, pair = DK * (h % 2), h // 2
                    kvp = PS[0][p0:p0 + DK, c % 2, h * DV:(h + 1) * DV]
                    if c == 0:
                        dve.tensor_copy(state[p0:p0 + DK, 0, pair, :], kvp).then_inc(st_s, 1)
                    else:
                        if h == 0:
                            dve.wait_ge(st_s, H * c)
                        dve.scalar_tensor_tensor(out=state[p0:p0 + DK, c, pair, :], in0=state[p0:p0 + DK, c - 1, pair, :],
                                                 scalar=small[p0:p0 + DK, pair * NC_ + c:pair * NC_ + c + 1], in1=kvp,
                                                 op0=ALU.mult, op1=ALU.add).then_inc(st_s, 1)
            for r in range(NR):
                out_evac(r)
            for h in range(H):
                if h >= 1:
                    dve.wait_ge(ov_s, 2 * h)
                vv = v_smp[:, h * DV:(h + 1) * DV].unsqueeze(1).broadcast_to([NS, NS, DV])
                eye = ident[0:NS, 0:NS].unsqueeze(2).broadcast_to([NS, NS, DV])
                dve.tensor_tensor(x_bd[:, :].rearrange("p (s v) -> p s v", s=NS), vv, eye, ALU.mult).then_inc(vb_s, 1)
                for g in range(2):
                    dve.wait_ge(ov_s, 2 * h + g + 1)
                    p0, pair = DK * (h % 2), h // 2
                    dst = st_smp[p0:p0 + DK, pair, 4 * g:4 * g + 4, :].rearrange("p s v -> p (s v)")
                    dve.tensor_tensor(dst, dst, M[1][p0:p0 + DK, :], ALU.add).then_inc(stn_s, 1)
            dve.wait_ge(os_s, 1)
            for par_ in range(2):
                dve.tensor_copy(o_t[:, :, 0:NS].rearrange("p (a b) s -> p a b s", b=2)[:, :, par_, :],
                                M[par_][:, 0:2 * NS].rearrange("p (a s) -> p a s", a=2)).then_inc(osr_s, 1)
            for h in range(H):
                dve.wait_ge(grs_s, h + 1)
                dve.scalar_tensor_tensor(out=o_t[:, h, :], in0=o_t[:, h, :], scalar=par[:, P_GLAG:P_GLAG + 1],
                                         in1=tmp[:, 1, :], op0=ALU.mult, op1=ALU.mult).then_inc(gm_s, 1)
                dve.wait_ge(silu_s, h + 1)
                dve.wait_ge(gm_s, 3 * h + 1)
                dve.tensor_tensor(o_t[:, h, :], o_t[:, h, :], r_t[:, h, :], ALU.mult).then_inc(gm_s, 1)
                low(a_op[:, CT + h, 1, :], o_t[:, h, :], None, a_op[:, CT + h, 0, :], op_hi, 20 + h + 1).then_inc(op_lo, 1)
                dve.engine_nop().then_inc(gm_s, 1)

            def residual_tile(t, m, gain, n_op, n_sq):
                dve.wait_ge(tile_done, t + 1)
                dve.tensor_tensor(cols(x_res[:, m, :]), cols(x_res[:, m, :]), pcols(t % 2), ALU.add).then_inc(ps_free, 1)
                if gain is not None:
                    low(b_op[:, m, 1, :], x_res[:, m, :], par[:, gain + m:gain + m + 1], b_op[:, m, 0, :],
                        op_hi, n_op + m + 1).then_inc(op_lo, 1)
                dve.wait_ge(sq_s, n_sq + m + 1)
                if m == 0:
                    dve.engine_nop().then_inc(acc_s, 1)
                else:
                    dve.wait_ge(acc_s, n_sq + m)
                    dve.tensor_tensor(acc[:, :], acc[:, :], tmp[:, m % 2, :], ALU.add).then_inc(acc_s, 1)

            dve.wait_ge(xld, 16)
            for m in range(KT):
                residual_tile(T_OUT + m, m, G_XA, 24, 9)

            def kv_low(h):
                dve.wait_ge(kv_hi, h + 1)
                dve.tensor_tensor(kv[:, h % 2, 1, :, :], kv_raw[:, :, :], kv[:, h % 2, 0, :, :].bitcast(F32),
                                  ALU.subtract).then_inc(kv_lo, 1)

            def q_tiles(h):
                for j in range(2):
                    t = T_XQ + 2 * h + j
                    dve.wait_ge(tile_done, t + 1)
                    if t == T_XQ:
                        dve.wait_ge(rstd_s, 3)
                    if h >= 1:
                        dve.wait_ge(q_lo, 2 * h)
                    dve.tensor_tensor(cols(tmp[:, j, :]), pcols(t % 2), cols(rstd[:, :]), ALU.mult).then_inc(ps_free, 1)
                    low(a_op[:, 2 * h + j, 1, :], tmp[:, j, :], None, a_op[:, 2 * h + j, 0, :], q_hi, 2 * h + j + 1).then_inc(q_lo, 1)
                    link(dve.tensor_copy(small[:, 64 + 8 * (2 * h + j):72 + 8 * (2 * h + j)], tmp[:, j, 0:NS]))

            q_tiles(0)
            kv_low(0)
            for h in range(H):
                def chunk_scale(c):
                    dve.wait_ge(e_s, NC_ * h + c + 1)
                    link(dve.reciprocal(small[:, 40 + c:41 + c], small[:, 40 + c:41 + c]))
                    dve.tensor_scalar(ex[:, c, :], ex[:, c, :], small[:, 40 + c:41 + c], None, ALU.mult).then_inc(p_s, 1)

                for c in range(NC_):
                    dve.wait_ge(qk_s, NC_ * h + c + 1)
                    link(dve.tensor_reduce(small[:, 32 + c:33 + c], M[c % 2][:, 0:MEM], AX, ALU.max))
                    dve.tensor_scalar(small[:, 32 + c:33 + c], small[:, 32 + c:33 + c], -(HD ** -0.5), None,
                                      ALU.mult).then_inc(nm_s, 1)
                    if c >= 1:
                        chunk_scale(c - 1)
                chunk_scale(NC_ - 1)
                if h + 1 < H:
                    kv_low(h + 1)
                    q_tiles(h + 1)
                for u in range(2):
                    dve.wait_ge(pt_hi, 2 * h + u + 1)
                    dve.tensor_tensor(pt[:, :, 1, :], PS[u][:, 0:2, :], pt[:, :, 0, :].bitcast(F32),
                                      ALU.subtract).then_inc(pt_lo, 1)
                for u in range(2):
                    for d in range(2):
                        dve.wait_ge(oh_s, 4 * h + 2 * u + d + 1)
                        src = PS[u][:, 2, :] if d == 0 else M[u][:, :]
                        c0 = NS + 512 * u
                        dve.tensor_tensor(a_op[:, 2 * h + d, 1, c0:c0 + 512], src,
                                          a_op[:, 2 * h + d, 0, c0:c0 + 512].bitcast(F32), ALU.subtract).then_inc(ol_s, 1)
            dve.wait_ge(tile_done, T_XO)
            link(dve.memset(qz[:, :, :], 0.0))
            dve.memset(pz[:, :, :, :], 0.0).then_inc(pz_s, 1)
            qd = qz[:, :, 32:288].rearrange("p k (s n) -> p k s n", n=32)[:, :, :, 0]
            dve.tensor_copy(qd, small[:, 64:128].rearrange("p (k s) -> p k s", s=NS)).then_inc(qz_s, 1)
            dve.wait_ge(cu, NS)
            link(dve.tensor_reduce(small[0:32, 32:33], M[0][0:32, 0:MEM], AX, ALU.max))
            dve.tensor_scalar(small[0:32, 32:33], small[0:32, 32:33], -(HD ** -0.5), None, ALU.mult).then_inc(sm_s, 1)
            dve.wait_ge(se_s, 1)
            link(dve.reciprocal(small[0:32, 40:41], small[0:32, 40:41]))
            dve.tensor_scalar(ex[0:32, 0, :], ex[0:32, 0, :], small[0:32, 40:41], None, ALU.mult).then_inc(sp_s, 1)
            dve.wait_ge(spt, 1)
            for mt in range(2):
                dst = pz[:, mt, :, 8:72].rearrange("p h (s n) -> p h s n", n=8)[:, :, :, 0]
                dve.tensor_copy(dst, M[1][:, mt * 32:(mt + 1) * 32].rearrange("p (s h) -> p h s", h=H)).then_inc(pz_s, 1)
            dve.wait_ge(cu, 2 * NS)
            dve.tensor_copy(o_smp[:, 0:3 * HD].rearrange("p (h n) -> p h n", h=3), PS[0][0:NS, :, 0:HD]).then_inc(sor_s, 1)
            dve.tensor_copy(o_smp[:, 3 * HD:], PS[1][0:NS, 0, 0:HD]).then_inc(sor_s, 1)
            dve.wait_ge(soh, 1)
            dve.tensor_tensor(a_op[:, :, 1, 0:NS], M[0][:, 0:KT * NS].rearrange("p (k s) -> p k s", s=NS),
                              a_op[:, :, 0, 0:NS].bitcast(F32), ALU.subtract).then_inc(sol, 1)

            dve.wait_ge(xld, 32)
            for m in range(KT):
                residual_tile(T_XO + m, m, G_FF, 32, 17)

            def up(t, j, m, count):
                dve.wait_ge(tile_done, t + 1)
                dve.scalar_tensor_tensor(out=cols(tmp[:, j, :]), in0=pcols((T_FF + j) % 2), scalar=0.0,
                                         in1=cols(rstd[:, :]), op0=ALU.max, op1=ALU.mult).then_inc(ps_free, 1)
                dve.wait_ge(h_hi, count + 1)
                hi = a_op[:, bass.ds(m, 1), 0, :].rearrange("p a n -> p (a n)").bitcast(F32)
                dst = a_op[:, bass.ds(m, 1), 1, :].rearrange("p a n -> p (a n)")
                dve.tensor_tensor(dst, tmp[:, j, :], hi, ALU.subtract).then_inc(h_lo, 1)

            def down(t, j, m):
                dve.wait_ge(tile_done, t + 1)
                x = x_res[:, bass.ds(m, 1), :].rearrange("p a (b c) -> p (a b) c", b=NB)
                dve.tensor_tensor(x, x, pcols((T_FF + j) % 2), ALU.add).then_inc(ps_free, 1)

            dve.wait_ge(rstd_s, 4)
            dve.wait_ge(acc_s, 25)
            with dve.Fori(0, FG - 1) as g:
                with dve.Fori(0, KT // 2) as i:
                    for j in range(2):
                        up(g * 16 + i * 2 + (T_FF + j), j, i * 2 + j, g * 8 + i * 2 + (j + 0))
                with dve.Fori(0, KT // 2) as i:
                    for j in range(2):
                        down(g * 16 + i * 2 + (T_FF + KT + j), j, i * 2 + j)
            g = FG - 1
            with dve.Fori(0, KT // 2) as i:
                for j in range(2):
                    up(i * 2 + (T_FF + 16 * g + j), j, i * 2 + j, i * 2 + (g * 8 + j))
            for m in range(KT):
                residual_tile(T_FF + 16 * g + KT + m, m, None, 0, 25)
            dve.wait_ge(rstd_s, 5)
            for m in range(KT):
                dve.scalar_tensor_tensor(out=x_res[:, m, :], in0=x_res[:, m, :], scalar=par[:, G_FIN + m:G_FIN + m + 1],
                                         in1=rstd[:, :], op0=ALU.mult, op1=ALU.mult).then_inc(y_out, 1)


def kernel(x_prompt, x_sample, cache_conv, state_gla, cache_mem_k, cache_mem_v, mem_prompt, norm_mix_g, w_in,
           w_alpha, b_alpha, w_dw, b_dw, conv_ln_g, conv_ln_b, gla_norm_g, w_out, norm_xa_g, mem_norm_g, w_xq,
           w_xk, w_xv, w_xo, norm_ffn_g, w_up, w_down, final_g):
    import numpy as np
    import concourse.bacc as bacc
    from concourse.bass_utils import run_bass_kernel_spmd as run

    f32 = np.float32

    def tiles(w):
        w = np.asarray(w)
        k, n = w.shape
        return w.reshape(k // D, KT, P, n // P, P).transpose(3, 0, 2, 1, 4)

    def feat(v):
        return np.asarray(v).reshape(-1, P).T

    w = np.asarray(w_in)[0]
    cv, cg, qq, kk, vv, rr, aa = np.split(w, [512, 1024, 1280, 1536, 2048, 2560], axis=1)
    conv = np.stack([cv.reshape(D, CT, P), cg.reshape(D, CT, P)], axis=2).reshape(D, 2 * DC)
    a_pad = np.concatenate([aa, np.zeros((D, P - RANK), f32)], axis=1)
    w_in_r = np.concatenate([conv, a_pad, kk, qq, vv, rr], axis=1)
    parts = [tiles(m)[:, 0] for m in (w_xk[0], w_xv[0], w_in_r, w_out[0], w_xq[0], w_xo[0])]
    up, down = tiles(w_up[0])[:, 0], tiles(w_down[0])
    for g in range(FG):
        parts += [up[g * KT:(g + 1) * KT], down[:, g]]
    wt = np.concatenate(parts, axis=0)

    x = np.concatenate([np.asarray(x_sample)[:, 0], np.asarray(x_prompt)[0]], axis=0)
    wdw = np.asarray(w_dw)[0].T.reshape(CT, P, CW).transpose(1, 0, 2).reshape(P, CT * CW)
    par = np.concatenate([feat(mem_norm_g[0]), feat(norm_mix_g[0]), feat(norm_xa_g[0]), feat(norm_ffn_g[0]),
                          feat(final_g), feat(b_dw[0]), feat(conv_ln_g[0]), feat(conv_ln_b[0]),
                          feat(gla_norm_g[0]), feat(b_alpha[0]), wdw], axis=1)
    cc = np.asarray(cache_conv)[0].reshape(NS, CW - 1, CT, P).transpose(3, 2, 0, 1)
    cc = np.concatenate([cc, np.zeros((P, CT, NS, 1), f32)], axis=3)
    arrays = {
        "wt": wt,
        "x": x.T.reshape(KT, P, T).transpose(1, 0, 2),
        "mem": np.asarray(mem_prompt)[0].T.reshape(KT, P, MEM).transpose(1, 0, 2),
        "par": par,
        "w_alpha": np.asarray(w_alpha)[0],
        "conv_cache": cc,
        "state": np.asarray(state_gla)[0].reshape(NS, 2, 2, DK, DV).transpose(2, 3, 1, 0, 4).reshape(P, 2, NS, DV),
        "cache_k": np.asarray(cache_mem_k)[0].reshape(NS, MEM, KT, P).transpose(0, 3, 2, 1).reshape(NS, P, KT * MEM),
        "cache_v": np.asarray(cache_mem_v)[0].reshape(NS, 2, P, D).transpose(0, 2, 1, 3).reshape(NS, P, 2 * D),
    }
    outs = {"y": (P, KT, T), "mk": (P, KT, MEM), "mv": (P, 2, D), "conv_p": (P, CT, CW - 1),
            "conv_s": (P, CT, NS, CW - 1), "gla_p": (P, 2, DV), "gla_s": (P, 2, NS, DV)}

    nc = bacc.Bacc("TRN2", target_bir_lowering=False, num_devices=1)
    arrays = {k: np.ascontiguousarray(v) for k, v in arrays.items()}
    ins = {k: nc.dram_tensor(f"in_{k}", v.shape, F32, kind="ExternalInput").ap() for k, v in arrays.items()}
    out = {k: nc.dram_tensor(f"out_{k}", v, F32, kind="ExternalOutput").ap() for k, v in outs.items()}
    build(nc, ins, out)
    r = run(nc, [{f"in_{k}": v for k, v in arrays.items()}], core_ids=[0]).results[0]
    r = {k: np.asarray(r[f"out_{k}"]) for k in outs}

    y = r["y"].transpose(2, 1, 0).reshape(T, D)
    return (y[NS:].reshape(1, SEQ, D), y[:NS].reshape(NS, 1, D),
            r["conv_p"].transpose(2, 1, 0).reshape(1, 1, CW - 1, DC),
            r["conv_s"].transpose(2, 3, 1, 0).reshape(1, NS, CW - 1, DC),
            r["gla_p"].reshape(2, DK, 2, DV).transpose(2, 0, 1, 3).reshape(1, 1, H, DK, DV),
            r["gla_s"].reshape(2, DK, 2, NS, DV).transpose(3, 2, 0, 1, 4).reshape(1, NS, H, DK, DV),
            r["mk"].transpose(2, 1, 0).reshape(1, 1, MEM, H, HD),
            r["mv"].transpose(1, 0, 2).reshape(1, 1, MEM, H, HD))
```

```python
from contextlib import ExitStack

import concourse.bass as bass
from concourse import mybir

F32 = mybir.dt.float32
F32R = mybir.dt.float32r
I8 = mybir.dt.int8
ALU = mybir.AluOpType
ACT = mybir.ActivationFunctionType
AX = mybir.AxisListType.X

P = 128
D = 1024
KT = D // P
SEQ = 1024
NS = 8
T = NS + SEQ
NB = 3
CB = T // NB
MEM = 256
EPS = 1e-6
DC = 512
CT = DC // P
CW = 31
H = 4
DK = 64
DV = 128
RANK = 16
TAU = 16.0
C = 128
NC_ = SEQ // C
HD = 256
FG = 4

T_KV = 0
T_IN = 16
N_IN = 21
I_A, I_K, I_Q, I_V, I_R = 8, 9, 11, 13, 17
T_OUT = T_IN + N_IN
T_XQ = T_OUT + KT
T_XO = T_XQ + KT
T_FF = T_XO + KT
N_T = T_FF + FG * 2 * KT
LEVELS = (1, 2, 4, 8, 16, 32, 64)
N_TAPS = CT * CW

ORDER = [("kv", n) for n in range(4)]
for _i in range(12):
    ORDER += [("in", _i), ("kv", 4 + _i)]
ORDER += [("in", _i) for _i in range(12, N_IN)]
PLACE = {what: t for t, what in enumerate(ORDER)}
assert len(ORDER) == T_OUT

N_UNITS = 2 * (len(LEVELS) + 1)
_PLACES = [(I_V + 3, 5), (I_V + 3, 7)] + [(i, k) for i in (I_R, I_R + 1, I_R + 2) for k in (1, 3, 5, 7)] + [
    (I_R + 3, 1), (I_R + 3, 3)]
UNITS_IN = {}
for _u, (_i, _k) in enumerate(_PLACES):
    UNITS_IN.setdefault(PLACE["in", _i], []).append((_k, _u))

AFTER = {}
for _g in range(4):
    AFTER.setdefault(PLACE["kv", 9 + 2 * _g] + 1, []).append(("mv", _g))
AFTER.setdefault(PLACE["in", I_K], []).extend(("z", j) for j in range(2 * NB))
for _m in range(4):
    AFTER.setdefault(PLACE["in", I_V + _m + 1], []).extend(("v", _m, g) for g in range(3))
AFTER[PLACE["in", I_V + 1]].extend(("mean", b) for b in range(NB))
AFTER[PLACE["in", I_V + 2]].extend(("var", b) for b in range(NB))
AFTER[T_OUT - 1] = [("kt", g) for g in range(4)] + [("smp", 0)]
MISC = {name: n for n, name in enumerate(
    name for p in range(T_OUT)
    for name in [("unit", u, g) for _, u in UNITS_IN.get(p, ()) for g in range(2)] + AFTER.get(p, []))}

TAPS_DVE = [(m, w) for m in (0, 2, 3) for w in range(CW)]
TAPS_POOL = [(1, w) for w in range(CW)]


def taps_after(p):
    def upto(q):
        first, last = PLACE["in", 1] + 1, PLACE["in", 12]
        d = 0 if q < first else len(TAPS_DVE) if q >= last else (q - first + 1) // 2 * 8 + (7 if (q - first) % 2 == 0 else 0)
        first, mid = PLACE["in", 3] + 1, PLACE["in", 8] + 2
        g = 0 if q < first else (q - first + 1) * 3 // 2 if q < mid else (mid - first) * 3 // 2 + 2 * (q - mid + 1)
        return min(d, len(TAPS_DVE)), min(g, len(TAPS_POOL))
    (d0, g0), (d1, g1) = upto(p - 1), upto(p)
    return (d0, d1), (g0, g1)


G_MEM, G_MIX, G_XA, G_FF, G_FIN = 0, 8, 16, 24, 32
P_BDW, P_LNG, P_LNB, P_GLAG, P_BAL = 40, 44, 48, 52, 53
P_WDW = 55
NPAR = P_WDW + CT * CW


def build(nc, a, o):
    names = ExitStack()
    with names:
        base = (nc.sbuf_base + 31) // 32 * 32

        def at(name, offset, shape, dt=F32):
            return nc.alloc_sbuf_tensor_at(name, shape, dt, offset=base + offset)

        def sem(name):
            return names.enter_context(nc.semaphore(name))

        SPLIT = KT * 2 * T * 4
        a_op = at("a_op", 0, [P, KT, 2, T], F32R)
        o1 = SPLIT
        w_split = at("w_split", o1, [P, 2, 2, KT, P], F32R)
        o1 += 2 * 2 * KT * P * 4
        w_raw = at("w_raw", o1, [P, 2, KT, P])
        o1 += 2 * KT * P * 4
        rstd = at("rstd", o1, [P, T])
        o1 += T * 4
        acc = at("acc", o1, [P, T])
        a_lr = at("a_lr", o1, [RANK, T])
        kv_raw = at("kv_raw", o1, [P, 4, MEM])
        o1 += T * 4
        tmp = at("tmp", o1, [P, 2, T])
        lnz = tmp[:, :, :]
        o1 += 2 * T * 4
        ident = at("ident", o1, [P, P])
        ones = at("ones", o1 + 512, [P, P])
        par = at("par", o1 + 1024, [P, NPAR])
        o2 = o1 + 1024 + (NPAR * 4 + 31) // 32 * 32
        mask = at("mask", o2, [P, len(LEVELS) + 1, P], I8)
        o2 += 1024
        walpha = at("walpha", o2, [RANK, 2 * P])
        o2 += 1024
        small = at("small", o2, [P, 192])
        o2 += 768
        m_rstd = at("m_rstd", o2, [P, MEM])
        o2 += MEM * 4
        o1 = (o2 + 31) // 32 * 32

        b_op = at("b_op", o1, [P, KT, 2, T], F32R)
        x_res = at("x_res", o1 + SPLIT, [P, KT, T])
        o_u, o_cs = o1, o1 + CT * (CW - 1 + SEQ) * 4
        o_y = o_cs + 4096
        o_q = o_y + CT * T * 4
        o_k = o_q + 2 * T * 4
        o_z = o_k + 2 * T * 4
        o_v = o_z + 2 * T * 4
        o_r = o_v + NC_ * DC * 4
        o_sm = o_r + H * T * 4
        conv_in = at("conv_in", o_u, [P, CT, CW - 1 + SEQ])
        conv_smp = at("conv_smp", o_cs, [P, CT, NS, CW])
        conv_y = at("conv_y", o_y, [P, CT, T])
        q_t = at("q_t", o_q, [P, 2, T])
        k_t = at("k_t", o_k, [P, 2, T])
        la = at("la", o_z, [P, 2, T])
        v_tok = at("v_tok", o_v, [P, NC_, DC])
        r_t = at("r_t", o_r, [P, H, T])
        keep = at("keep", o_sm, [P, SEQ], I8)
        v_smp = at("v_smp", o_sm + SEQ, [NS, DC])
        assert o_sm + SEQ + DC * 4 <= o1 + SPLIT + KT * T * 4
        x_in = at("x_in", o_y, [P, KT, T])
        m_op = at("m_op", o_v, [P, KT, 2, MEM], F32R)
        m_raw = at("m_raw", o_r, [P, KT, MEM])
        prod = at("prod", o_r, [P, 2, T])
        mvt = at("mvt", o_r + 2 * T * 4, [P, 2, 2, MEM])
        m_out = at("m_out", o_r + 3 * T * 4, [P, 2, 2, MEM])
        msq = at("msq", o_z, [P, KT, MEM])
        sc_t = at("sc_t", o_u, [P, 2, NC_, 2, C])
        qz = [acc[:, 0:SEQ], at("qz1", o_cs, [P, SEQ])]
        k_in = at("k_in", o_k, [P, NC_, 2, P])
        state = at("state", o_z, [P, NC_, 2, DV])
        sq_t = at("sq_t", (KT - 2) * 2 * T * 4, [P, H, T])
        lnv = at("lnv", o_q, [P, H, T])
        st_smp = tmp[:, :, 0:SEQ]
        vb = [acc[:, 0:NS * DV], at("vb1", o_cs, [P, NS * DV])]
        ox = o1 + SPLIT
        kv = at("kv", ox, [P, 2, 2, 4, MEM], F32R)
        pt = at("pt", ox + 16384, [P, 2, 2, 512], F32R)
        ex = at("ex", ox + 24576, [P, NC_, MEM])
        qzs = at("qzs", o1, [P, KT, 320])
        pz = at("pz", o1 + KT * 320 * 4, [P, 2, H, 80])
        o_cache = o1 + KT * 320 * 4 + 2560
        NCS = 6
        cache = [at(f"cache{i}", o_cache + 8192 * i, [P, KT * MEM]) for i in range(NCS)]
        assert o_cache + 8192 * NCS <= o1 + SPLIT - 4096
        o_smp = at("o_smp", o1 + SPLIT - 4096, [NS, D])

        PS = [names.enter_context(nc.psum_tensor(f"ps{i}", [P, NB, 512], F32)) for i in range(2)]
        M = [names.enter_context(nc.psum_tensor(f"m{i}", [P, 512], F32)) for i in range(2)]

        x_part = [sem(f"x_part{i}") for i in range(4)]
        m_part = [sem(f"m_part{i}") for i in range(2)]
        misc_full = [sem("misc_full0"), sem("misc_full1")]
        misc_free = [sem("misc_free0"), sem("misc_free1")]
        prod_s, pool_tap, dve_tap = sem("prod_s"), sem("pool_tap"), sem("dve_tap")
        conv_st, conv_lo, gla_lo = sem("conv_st"), sem("conv_lo"), sem("gla_lo")
        zero_s, qzero = sem("zero_s"), sem("qzero")
        goo_s = sem("goo_s")
        vsp, vb_in, smp_s = sem("vsp"), sem("vb_in"), sem("smp_s")
        kx_s2, xr = sem("kx_s2"), [sem("xr0"), sem("xr1")]
        par_in, x_in_s, wa_in, cs_in, st_in = (sem(n) for n in ("par_in", "x_in_s", "wa_in", "cs_in", "st_in"))
        consts, eps_s = sem("consts"), sem("eps_s")
        w_in = [sem("w_in0"), sem("w_in1")]
        w_hi, w_lo = sem("w_hi"), sem("w_lo")
        tile_done = sem("tile_done")
        ps_free = sem("ps_free")
        op_hi, op_lo = sem("op_hi"), sem("op_lo")
        sq_s, acc_s = sem("sq_s"), sem("acc_s")
        sum_s, sumr_s, rstd_s = sem("sum_s"), sem("sumr_s"), sem("rstd_s")
        link_v, link_a, link_g = sem("link_v"), sem("link_a"), sem("link_g")
        out_s = sem("out_s")
        mv_t, mv_c = sem("mv_t"), sem("mv_c")
        gst = sem("gst")
        kvst = sem("kvst")
        sig_s, u_s, silu_s = sem("sig_s"), sem("u_s"), sem("silu_s")
        alr_s, z_s, zr_s, soft_s = sem("alr_s"), sem("z_s"), sem("zr_s"), sem("soft_s")
        vt_s, vr_s = sem("vt_s"), sem("vr_s")
        y_s, ln_s, lnr_s, mean_s, lsq_s, lacc_s, ysil_s = (sem(n) for n in ("y_s", "ln_s", "lnr_s", "mean_s", "lsq_s", "lacc_s", "ysil_s"))
        yn_s = sem("yn_s")
        lsub_s, lexp_s, lev_s, pp_s, sel_s = (sem(n) for n in ("lsub_s", "lexp_s", "lev_s", "pp_s", "sel_s"))
        qk_in_s, kx_s, qi_s, kt_s, ktr_s, kvp_s, dec_s, st_s, go_s, gor_s = (sem(n) for n in (
            "qk_in_s", "kx_s", "qi_s", "kt_s", "ktr_s", "kvp_s", "dec_s", "st_s", "go_s", "gor_s"))
        ks_s, ksr_s, vb_s, ov_s, stn_s, os_s, osr_s, sdec_s = (sem(n) for n in (
            "ks_s", "ksr_s", "vb_s", "ov_s", "stn_s", "os_s", "osr_s", "sdec_s"))
        gsq_s, gn_s, gnr_s, grs_s, gm_s = (sem(n) for n in ("gsq_s", "gn_s", "gnr_s", "grs_s", "gm_s"))
        xld, xsp = sem("xld"), sem("xsp")
        q_hi, q_lo = sem("q_hi"), sem("q_lo")
        kvr, kv_hi, kv_lo = sem("kvr"), sem("kv_hi"), sem("kv_lo")
        qk_s, nm_s, e_s, p_s, ptd, pt_hi, pt_lo, pv_s, oh_s, ol_s = (sem(n) for n in (
            "qk_s", "nm_s", "e_s", "p_s", "ptd", "pt_hi", "pt_lo", "pv_s", "oh_s", "ol_s"))
        ca = [sem(f"ca{i}") for i in range(NCS)]
        qz_s, ks2, sm_s, se_s, sp_s, spt, pz_s, cu, so_s, sor_s, sot, soh, sol = (sem(n) for n in (
            "qz_s", "ks2", "sm_s", "se_s", "sp_s", "spt", "pz_s", "cu", "so_s", "sor_s", "sot", "soh", "sol"))
        h_hi, h_lo = sem("h_hi"), sem("h_lo")
        y_out = sem("y_out")

        def cols(ap):
            return ap.rearrange("p (b c) -> p b c", b=NB)

        def pcols(i):
            return PS[i][:, :, 0:CB]

        def prompt(t2):
            return t2[:, :, NS:T]

        def o_cols(h):
            return small[:, 160:192].rearrange("p (a s b) -> p a s b", a=2, b=2)[:, h // 2, :, h % 2]

        NR = NC_ // 2

        def misc(name):
            n = MISC[name]
            return M[n % 2], n % 2, n // 2

        def wait_full(eng, name):
            _, b, n = misc(name)
            eng.wait_ge(misc_full[b], n + 1)

        def wait_read(eng, name):
            _, b, n = misc(name)
            eng.wait_ge(misc_free[b], n + 1)

        def unit(u):
            return u // 2, u % 2, 0 if u < 2 else LEVELS[u // 2 - 1]

        def mul_count(u):
            return 2 * (u + 1) if u < 2 else 4 + 3 * (u - 1)

        def even_odd(ap, s):
            v = ap.rearrange("p (n e s) -> p n e s", e=2, s=s)
            return v[:, :, 0, :], v[:, :, 1, :]

        go_bank = [[PS[1][:, 0, :], PS[1][:, 1, :]], [PS[1][:, 2, :], PS[0][:, 2, :]]]
        WT = a["wt"]
        v_spill = nc.dram_tensor("v_spill", (NS, DC), F32, kind="Internal").ap()
        x_spill = nc.dram_tensor("x_spill", (P, KT, T), F32, kind="Internal").ap()
        block = names.enter_context(nc.Block())

        @block.sync
        def _(sp):
            sp.dma_start(m_raw[:, 0:4, :], a["mem"][:, 0:4, :]).then_inc(m_part[0], 16)
            sp.dma_start(par[:, :], a["par"]).then_inc(par_in, 16)

            def load_w(t, slot, wait=True):
                if wait:
                    sp.wait_ge(w_lo, t * 2 - 2)
                src = WT[t] if isinstance(t, int) else WT[bass.ds(t, 1)].rearrange("a p k n -> (a p) k n")
                sp.dma_start(w_raw[:, slot, :, :], src).then_inc(w_in[slot], 16)

            load_w(0, 0, False)
            sp.dma_start(m_raw[:, 4:8, :], a["mem"][:, 4:8, :]).then_inc(m_part[1], 16)
            load_w(1, 1, False)
            for t in range(2, T_XO + 2):
                load_w(t, t % 2)
                for q in range(4):
                    if t == PLACE["kv", 2 * q + 1] + 4:
                        sp.wait_ge(ps_free, PLACE["kv", 2 * q + 1] + 1)
                        sp.dma_start(o["mk"][:, 2 * q:2 * q + 2, :], m_out[:, q % 2, :, :]).then_inc(kvst, 16)
                    if t == PLACE["kv", 9 + 2 * q] + 5:
                        wait_read(sp, ("mv", q))
                        sp.dma_start(o["mv"][:, :, 256 * q:256 * (q + 1)], m_out[:, q % 2, :, :]).then_inc(kvst, 16)
                if t == PLACE["in", 7] + 4:
                    sp.wait_ge(u_s, 2 * CT)
                    sp.dma_start(o["conv_p"], conv_in[:, :, SEQ:]).then_inc(conv_st, 16)
                    sp.dma_start(o["conv_s"], conv_smp[:, :, :, 1:]).then_inc(conv_st, 16)
                if t == T_OUT + 1:
                    wait_read(sp, ("v", 3, 2))
                    sp.dma_start(v_spill, v_smp[:, :]).then_inc(vsp, 16)
                if t == T_OUT + 2:
                    sp.wait_ge(vsp, 16)
                    wait_full(sp, ("unit", N_UNITS - 1, 1))
                    for pair in range(2):
                        for par_ in range(2):
                            h = 2 * pair + par_
                            sp.dma_start(vb[pair][DK * par_:DK * (par_ + 1), :].rearrange("p (s v) -> p s v", s=NS),
                                         v_spill[:, h * DV:(h + 1) * DV].unsqueeze(0).broadcast_to([DK, NS, DV])
                                         ).then_inc(vb_in, 16)
                    wait_full(sp, ("kt", 3))
                    sp.dma_start(st_smp.rearrange("p a (s v) -> p a s v", s=NS), a["state"]).then_inc(st_in, 16)
                    sp.wait_ge(st_s, H * NC_)
                    sp.dma_start(o["gla_p"], state[:, NC_ - 1, :, :]).then_inc(gst, 16)
                    sp.wait_ge(stn_s, 2)
                    sp.dma_start(o["gla_s"], st_smp.rearrange("p a (s v) -> p a s v", s=NS)).then_inc(gst, 16)
                    sp.wait_ge(gm_s, 3 * H)
                    sp.dma_start(x_res[:, 0:2, :], a["x"][:, 0:2, :]).then_inc(xr[0], 16)
                    sp.dma_start(x_res[:, 2:KT, :], a["x"][:, 2:KT, :]).then_inc(xr[1], 16)
                if T_OUT + 3 <= t < T_XQ + 3:
                    m = t - T_OUT - 3
                    sp.wait_ge(ps_free, T_OUT + m + 1)
                    sp.dma_start(x_spill[:, m, :], x_res[:, m, :]).then_inc(xsp, 16)
                if t in (T_XQ + 3, T_XQ + 5, T_XQ + 7, T_XQ + 9):
                    h = (t - T_XQ - 3) // 2
                    if h == 0:
                        sp.wait_ge(kvst, 128)
                        sp.wait_ge(sumr_s, 7)
                    else:
                        sp.wait_ge(kv_lo, h)
                    sp.dma_start(kv_raw[:, 0:2, :], o["mk"][:, 2 * h:2 * h + 2, :]).then_inc(kvr, 16)
                    sp.dma_start(kv_raw[:, 2:4, :], o["mv"][:, :, h * HD:(h + 1) * HD]).then_inc(kvr, 16)
            sp.wait_ge(tile_done, T_XO)
            for r in range(2 * NS):
                if r >= NCS:
                    sp.wait_ge(cu, r - NCS + 1)
                src = a["cache_k"][r] if r < NS else a["cache_v"][r - NS]
                sp.dma_start(cache[r % NCS][:, :], src).then_inc(ca[r % NCS], 16)
            sp.wait_ge(pv_s, 4 * H)
            sp.wait_ge(spt, 1)
            sp.dma_start(x_res[:, :, :], x_spill[:, :, :]).then_inc(xld, 16)
            load_w(T_XO + 2, (T_XO + 2) % 2)
            first = T_XO + 3
            with sp.Fori(0, (N_T - first) // 2) as i:
                for j in range(2):
                    load_w(i * 2 + (first + j), (first + j) % 2)
            assert (N_T - first) % 2 == 1
            load_w(N_T - 1, (N_T - 1) % 2)

        @block.gpsimd
        def _(gp):
            n = 0

            def link(ins):
                nonlocal n
                n += 1
                ins.then_inc(link_g, 1)
                gp.wait_ge(link_g, n)

            link(gp.memset(ident[:, :], 0.0))
            link(gp.memset(ones[:, :], 1.0))
            link(gp.affine_select(out=ident[:, :], in_=ident[:, :], compare_op=ALU.not_equal, fill=1.0,
                                  base=0, pattern=[[-1, P]], channel_multiplier=1))
            link(gp.memset(mask[:, :, :], 1))
            even, odd = even_odd(mask[:, 0, :], 1)
            link(gp.memset(odd, 0))
            link(gp.affine_select(out=even, in_=even, compare_op=ALU.is_equal, fill=0.0,
                                  base=0, pattern=[[-2, C // 2], [0, 1]], channel_multiplier=1))
            for l, s in enumerate(LEVELS):
                even, odd = even_odd(mask[:, l + 1, :], s)
                link(gp.memset(even, 0))
                nb = C // (2 * s)
                link(gp.affine_select(out=odd, in_=odd, compare_op=ALU.is_ge, fill=0.0,
                                      base=0, pattern=[[-2 * s, nb], [0, s]], channel_multiplier=1))
                link(gp.affine_select(out=odd, in_=odd, compare_op=ALU.is_ge, fill=0.0,
                                      base=s if s == 1 else s - 1, pattern=[[2 * s, nb], [0, s]], channel_multiplier=-1))
            link(gp.memset(keep[:, :], 1))
            gp.memset(keep[:, :].rearrange("p (c n) -> p c n", n=C)[:, :, 0:1], 0).then_inc(consts, 1)

            def lo(t, slot):
                gp.wait_ge(w_hi, t + 1)
                for k in (0, KT // 2):
                    part = slice(k, k + KT // 2)
                    gp.tensor_tensor(w_split[:, slot, 1, part, :], w_raw[:, slot, part, :],
                                     w_split[:, slot, 0, part, :].bitcast(F32), ALU.subtract).then_inc(w_lo, 1)

            def level_sub(u):
                l, pair, s = unit(u)
                be, bo = even_odd(la[:, pair, NS:T], s)
                ee, eo = even_odd(tmp[:, pair, 0:SEQ], s)
                if u == 2:
                    gp.wait_ge(yn_s, CT)
                if u >= 4:
                    wait_full(gp, ("unit", u - 2, 1))
                if s == 1:
                    gp.tensor_tensor(ee, bo, be, ALU.subtract).then_inc(lsub_s, 1)
                    gp.memset(eo, 0.0).then_inc(lsub_s, 1)
                else:
                    end = be[:, :, s - 1:s].broadcast_to([P, SEQ // (2 * s), s])
                    gp.tensor_tensor(ee, end, be, ALU.subtract).then_inc(lsub_s, 1)
                    gp.tensor_tensor(eo, bo, end, ALU.subtract).then_inc(lsub_s, 1)

            lo(0, 0)
            lo(1, 1)
            for p in range(T_OUT):
                for _, u in UNITS_IN.get(p, ()):
                    if u >= 2 and u + 2 < N_UNITS:
                        level_sub(u + 2)
                lo(p + 2, p % 2)
                for j in range(*taps_after(p)[1]):
                    m, w = TAPS_POOL[j]
                    gp.wait_ge(prod_s, j + 1)
                    if w == 0:
                        gp.engine_nop().then_inc(pool_tap, 1)
                    else:
                        gp.wait_ge(pool_tap, j)
                        gp.tensor_tensor(conv_y[:, m, NS:T], conv_y[:, m, NS:T], prod[:, j % 2, 0:SEQ], ALU.add).then_inc(pool_tap, 1)
                if p == PLACE["in", I_V]:
                    gp.wait_ge(dve_tap, 1)
                    gp.wait_ge(conv_st, 32)
                    gp.memset(sc_t[:, :, :, :, :], 0.0).then_inc(zero_s, 1)
                if p == PLACE["in", I_V + 2]:
                    level_sub(2)
                    level_sub(3)
            for m in range(CT):
                gp.wait_ge(op_hi, 16 + m + 1)
                gp.tensor_tensor(a_op[:, m, 1, :], conv_y[:, m, :], a_op[:, m, 0, :].bitcast(F32), ALU.subtract).then_inc(conv_lo, 1)
            gp.wait_ge(dec_s, 2)
            gp.wait_ge(smp_s, 1)
            gp.wait_ge(vb_in, 64)
            for pair in range(2):
                kb = small[:, 64 + pair * NS:64 + (pair + 1) * NS].unsqueeze(2).broadcast_to([P, NS, DV])
                v3 = vb[pair][:, :].rearrange("p (s v) -> p s v", s=NS) if pair else vb[0].rearrange("p (s v) -> p s v", s=NS)
                gp.tensor_tensor(v3, v3, kb, ALU.mult).then_inc(vb_s, 1)
            gp.wait_ge(st_in, 16)
            for pair in range(2):
                db = small[:, 16 + pair * NS:16 + (pair + 1) * NS].unsqueeze(2).broadcast_to([P, NS, DV])
                s3 = st_smp[:, pair, :].rearrange("p (s v) -> p s v", s=NS)
                gp.tensor_tensor(s3, s3, db, ALU.mult).then_inc(vb_s, 1)
            for pair in range(2):
                gp.wait_ge(vb_s, 3 + pair)
                gp.tensor_tensor(st_smp[:, pair, :], st_smp[:, pair, :], vb[pair][:, :] if pair else vb[0], ALU.add).then_inc(stn_s, 1)
            assert T_OUT % 2 == 1
            lo(T_OUT + 2, 1)
            with gp.Fori((T_OUT + 3) // 2, N_T // 2) as i:
                lo(i * 2, 0)
                lo(i * 2 + 1, 1)
            lo(N_T - 1, (N_T - 1) % 2)

        @block.scalar
        def _(act):
            n = 0

            def link(ins):
                nonlocal n
                n += 1
                ins.then_inc(link_a, 1)
                act.wait_ge(link_a, n)

            def w_high(t, slot, count=None):
                if isinstance(t, int) and t >= N_T:
                    return
                act.wait_ge(w_in[slot], ((t // 2) if isinstance(t, int) else count) * 16 + 16)
                if not isinstance(t, int) or t >= 2:
                    act.wait_ge(tile_done, t - 1)
                act.activation(w_split[:, slot, 0, :, :], w_raw[:, slot, :, :], ACT.Copy).then_inc(w_hi, 1)

            def norm(k, n_sums, width=None):
                blocks = [(b * CB, CB) for b in range(NB)] if width is None else [(0, width)]
                for j, (c0, w) in enumerate(blocks):
                    act.wait_ge(sum_s, n_sums + j + 1)
                    act.activation(rstd[:, c0:c0 + w], M[j % 2][:, 0:w], ACT.Ln, bias=small[:, 128:129],
                                   scale=1.0 / D).then_inc(sumr_s, 1)
                act.wait_ge(sumr_s, n_sums + len(blocks))
                w = blocks[-1][0] + blocks[-1][1]
                act.activation(rstd[:, 0:w], rstd[:, 0:w], ACT.Exp, scale=-0.5).then_inc(rstd_s, 1)

            def load_x(i):
                act.dma_start(x_in[:, 2 * i:2 * i + 2, :], a["x"][:, 2 * i:2 * i + 2, :]).then_inc(x_part[i], 16)

            act.wait_ge(par_in, 16)
            load_x(0)
            for k in range(KT):
                if k % 4 == 0:
                    act.wait_ge(m_part[k // 4], 16)
                if k == 4:
                    w_high(0, 0)
                    for i in range(1, 4):
                        load_x(i)
                    act.dma_start(walpha[:, :], a["w_alpha"]).then_inc(wa_in, 16)
                    act.dma_start(conv_smp[:, :, :, :], a["conv_cache"]).then_inc(cs_in, 16)
                act.activation(m_op[:, k, 0, :], m_raw[:, k, :], ACT.Copy,
                               scale=par[:, G_MEM + k:G_MEM + k + 1]).then_inc(op_hi, 1)
            act.activation(msq[:, :, :], m_raw[:, :, :], ACT.Square).then_inc(sq_s, 1)
            w_high(1, 1)
            act.wait_ge(eps_s, 1)
            act.wait_ge(sum_s, 1)
            act.activation(m_rstd[:, :], M[0][:, 0:MEM], ACT.Ln, bias=small[:, 128:129], scale=1.0 / D).then_inc(sumr_s, 1)
            act.wait_ge(sumr_s, 1)
            act.activation(m_rstd[:, :], m_rstd[:, :], ACT.Exp, scale=-0.5).then_inc(rstd_s, 1)

            def square(src, dst_first, j, n0):
                if j == 0:
                    act.activation(acc[:, :], src, ACT.Square).then_inc(sq_s, 1)
                else:
                    if j >= 3:
                        act.wait_ge(acc_s, n0 + j - 1)
                    act.activation(tmp[:, j % 2, :], src, ACT.Square).then_inc(sq_s, 1)

            for k in range(KT):
                if k % 2 == 0:
                    act.wait_ge(x_part[k // 2], 16)
                act.activation(a_op[:, k, 0, :], x_in[:, k, :], ACT.Copy,
                               scale=par[:, G_MIX + k:G_MIX + k + 1]).then_inc(op_hi, 1)
                if k % 2 == 1:
                    w_high(2 + k // 2, (k // 2) % 2)
            for k in range(KT):
                square(x_in[:, k, :], None, k, 1)

            def level_exp(u):
                act.wait_ge(lsub_s, 2 * (u - 1))
                act.activation(tmp[:, u % 2, 0:SEQ], tmp[:, u % 2, 0:SEQ], ACT.Exp, scale=1.0 / TAU).then_inc(lexp_s, 1)

            def read(name, src, dst, **kw):
                bank, b, _ = misc(name)
                wait_full(act, name)
                act.activation(dst, src(bank), ACT.Copy, **kw).then_inc(misc_free[b], 1)

            for p in range(T_OUT):
                kind, i = ORDER[p]
                for _, u in UNITS_IN.get(p, ()):
                    if u >= 2 and u + 2 < N_UNITS:
                        level_exp(u + 2)
                if p == T_OUT - 1:
                    act.wait_ge(kx_s, 1)
                    act.activation(tmp[:, :, 0:SEQ], tmp[:, :, 0:SEQ], ACT.Exp, scale=1.0 / TAU).then_inc(kx_s2, 1)
                    last = prompt(la).rearrange("p a (c n) -> p a c n", n=C)[:, :, :, C - 1]
                    act.activation(small[:, 0:16].rearrange("p (a c) -> p a c", a=2), last, ACT.Exp,
                                   scale=1.0 / TAU).then_inc(dec_s, 1)
                    act.activation(small[:, 16:32].rearrange("p (a s) -> p a s", a=2), la[:, :, 0:NS], ACT.Exp,
                                   scale=1.0 / TAU).then_inc(dec_s, 1)
                    act.wait_ge(dec_s, 2)
                    act.activation(prompt(la), prompt(la), ACT.Exp, scale=1.0 / TAU).then_inc(kx_s2, 1)
                if p >= 4:
                    w_high(p + 2, p % 2)
                    if kind == "in" and i < 8 and i % 2 == 1:
                        act.wait_ge(ps_free, p + 1)
                        act.activation(tmp[:, 1, :], tmp[:, 1, :], ACT.Sigmoid).then_inc(sig_s, 1)
                    if p == 4:
                        norm(1, 1)
                for j in range(*taps_after(p)[1]):
                    m, w = TAPS_POOL[j]
                    tap = par[:, P_WDW + m * CW + w:P_WDW + m * CW + w + 1]
                    if j == 0:
                        act.wait_ge(u_s, 2 * m + 2)
                        act.wait_ge(op_lo, 16)
                    if j >= 2:
                        act.wait_ge(pool_tap, j - 1)
                    if w == 0:
                        act.activation(conv_y[:, m, NS:T], conv_in[:, m, w:w + SEQ], ACT.Identity,
                                       bias=par[:, P_BDW + m:P_BDW + m + 1], scale=tap).then_inc(prod_s, 1)
                    else:
                        act.activation(prod[:, j % 2, 0:SEQ], conv_in[:, m, w:w + SEQ], ACT.Copy, scale=tap).then_inc(prod_s, 1)
                if kind == "in" and i == I_K + 1:
                    wait_read(act, ("z", 4))
                    wait_read(act, ("z", 5))
                    link(act.activation(lnz, la[:, :, :], ACT.Abs))
                    link(act.activation(lnz, lnz, ACT.Exp, scale=-1.0))
                    act.activation(lnz, lnz, ACT.Ln, bias=1.0).then_inc(soft_s, 1)
                if kind == "in" and i >= I_R:
                    act.wait_ge(ps_free, p + 1)
                    act.activation(r_t[:, i - I_R, :], r_t[:, i - I_R, :], ACT.Silu).then_inc(silu_s, 1)
                for name in AFTER.get(p, ()):
                    if name[0] == "mv":
                        g = name[1]
                        act.wait_ge(kvst, 16 * (3 + g))
                        read(name, lambda b: b[:, :].rearrange("p (a n) -> p a n", a=2), m_out[:, g % 2, :, :])
                    if name[0] == "v" and name[2] < 2:
                        m, g = name[1:]
                        if m == 0:
                            act.wait_ge(tile_done, PLACE["kv", 15] + 1)
                        read(name, lambda b: b[:, :].rearrange("p (c n) -> p c n", c=4),
                             v_tok[:, 4 * g:4 * g + 4, m * P:(m + 1) * P])
                    elif name[0] == "v":
                        read(name, lambda b: b[0:NS, 0:P], v_smp[:, name[1] * P:(name[1] + 1) * P])
                    if name[0] == "mean":
                        j = name[1]
                        read(name, lambda b: b[:, 0:CB], tmp[:, 0, j * CB:(j + 1) * CB], scale=1.0 / DC)
                        if j == NB - 1:
                            for m in range(CT):
                                act.wait_ge(mean_s, m + 1)
                                if m >= 1:
                                    act.wait_ge(lacc_s, m)
                                dst = acc[:, :] if m == 0 else tmp[:, 1, :]
                                act.activation(dst, conv_y[:, m, :], ACT.Square).then_inc(lsq_s, 1)
                    if name[0] == "var":
                        j = name[1]
                        bank, b, _ = misc(name)
                        wait_full(act, name)
                        act.activation(tmp[:, 0, j * CB:(j + 1) * CB], bank[:, 0:CB], ACT.Ln,
                                       bias=small[:, 128:129], scale=1.0 / DC).then_inc(misc_free[b], 1)
                        if j == NB - 1:
                            wait_read(act, ("var", 1))
                            wait_read(act, ("var", 2))
                            act.activation(tmp[:, 0, :], tmp[:, 0, :], ACT.Exp, scale=-0.5).then_inc(lnr_s, 1)
                            level_exp(2)
                            level_exp(3)
                if p == PLACE["in", I_R]:
                    act.wait_ge(yn_s, CT)
                    for m in range(CT):
                        act.activation(conv_y[:, m, :], conv_y[:, m, :], ACT.Silu, bias=par[:, P_LNB + m:P_LNB + m + 1],
                                       scale=par[:, P_LNG + m:P_LNG + m + 1]).then_inc(ysil_s, 1)

            act.wait_ge(tile_done, T_OUT)
            for m in range(CT):
                act.wait_ge(ysil_s, m + 1)
                act.activation(a_op[:, m, 0, :], conv_y[:, m, :], ACT.Copy).then_inc(op_hi, 1)
            for g in range(4):
                act.wait_ge(qi_s, 1)
                read(("kt", g), lambda b: b[:, :].rearrange("p (c a n) -> p c a n", c=2, a=2), k_in[:, 2 * g:2 * g + 2, :, :])
            for r in range(NR):
                act.wait_ge(go_s, r + 1)
                act.activation(sc_t[:, :, 2 * r:2 * r + 2, 1, :], go_bank[r % 2][1][:, :].rearrange(
                    "p (c a n) -> p a c n", c=2, a=2), ACT.Copy).then_inc(goo_s, 1)
                act.wait_ge(goo_s, r + 1)
                act.wait_ge(gor_s, r + 1)
                for pair in range(2):
                    dst = sq_t[:, 2 * pair:2 * pair + 2, NS + 2 * C * r:NS + 2 * C * (r + 1)]
                    act.activation(dst.rearrange("p b (c n) -> p c b n", n=C), sc_t[:, pair, 2 * r:2 * r + 2, :, :],
                                   ACT.Square).then_inc(gsq_s, 1)
            act.wait_ge(osr_s, 1)
            for h in range(H):
                act.activation(sq_t[:, h, 0:NS], o_cols(h), ACT.Square).then_inc(gsq_s, 1)
            for h in range(H):
                for j in range(NB):
                    n_ = NB * h + j
                    act.wait_ge(gn_s, n_ + 1)
                    act.activation(lnv[:, h, j * CB:(j + 1) * CB], M[n_ % 2][:, 0:CB], ACT.Ln, bias=small[:, 128:129],
                                   scale=1.0 / DV).then_inc(gnr_s, 1)
            act.wait_ge(gn_s, NB * H)
            for h in range(H):
                act.wait_ge(gnr_s, NB * (h + 1))
                act.activation(sq_t[:, h, :], lnv[:, h, :], ACT.Exp, scale=-0.5).then_inc(grs_s, 1)
            for h in range(H):
                act.wait_ge(gm_s, 3 * (h + 1))
                if h >= 2:
                    act.wait_ge(gla_lo, h - 1 if h == 2 else h)
                act.activation(a_op[:, CT + h, 0, :], sq_t[:, h, :], ACT.Copy).then_inc(op_hi, 1)
            act.wait_ge(gst, 32)

            def residual_tile(t, m, gain, n_op, n_sq):
                act.wait_ge(ps_free, t + 1)
                if gain is not None:
                    act.activation(b_op[:, m, 0, :], x_res[:, m, :], ACT.Copy,
                                   scale=par[:, gain + m:gain + m + 1]).then_inc(op_hi, 1)
                square(x_res[:, m, :], None, m, n_sq)
                w_high(t + 2, (t + 2) % 2)

            for m in range(KT):
                residual_tile(T_OUT + m, m, G_XA, 24, 9)
            norm(2, 4)

            def kv_high(h):
                act.wait_ge(kvr, 32 * (h + 1))
                if h >= 2:
                    act.wait_ge(pv_s, 4 * (h - 1))
                act.activation(kv[:, h % 2, 0, :, :], kv_raw[:, :, :], ACT.Copy).then_inc(kv_hi, 1)

            def q_tiles(h):
                for j in range(2):
                    t = T_XQ + 2 * h + j
                    act.wait_ge(ps_free, t + 1)
                    act.activation(a_op[:, 2 * h + j, 0, :], tmp[:, j, :], ACT.Copy).then_inc(q_hi, 1)
                    w_high(t + 2, (t + 2) % 2)

            q_tiles(0)
            act.wait_ge(xsp, 16 * KT)
            kv_high(0)
            for h in range(H):
                for c in range(NC_):
                    if h >= 1 and c == 0:
                        act.wait_ge(ptd, 2 * h)
                    act.wait_ge(nm_s, NC_ * h + c + 1)
                    act.activation(ex[:, c, :], M[c % 2][:, 0:MEM], ACT.Exp, bias=small[:, 32 + c:33 + c],
                                   scale=HD ** -0.5, accum_out=small[:, 40 + c:41 + c]).then_inc(e_s, 1)
                if h + 1 < H:
                    kv_high(h + 1)
                    q_tiles(h + 1)
                for u in range(2):
                    act.wait_ge(ptd, 2 * h + u + 1)
                    if 2 * h + u >= 1:
                        act.wait_ge(pv_s, 2 * (2 * h + u))
                    act.activation(pt[:, :, 0, :], PS[u][:, 0:2, :], ACT.Copy).then_inc(pt_hi, 1)
                for u in range(2):
                    for d in range(2):
                        act.wait_ge(pv_s, 4 * h + 2 * u + d + 1)
                        src = PS[u][:, 2, :] if d == 0 else M[u][:, :]
                        act.activation(a_op[:, 2 * h + d, 0, NS + 512 * u:NS + 512 * (u + 1)], src,
                                       ACT.Copy).then_inc(oh_s, 1)
            act.wait_ge(sm_s, 1)
            act.activation(ex[0:32, 0, :], M[0][0:32, 0:MEM], ACT.Exp, bias=small[0:32, 32:33],
                           scale=HD ** -0.5, accum_out=small[0:32, 40:41]).then_inc(se_s, 1)
            act.wait_ge(sot, 1)
            act.activation(a_op[:, :, 0, 0:NS], M[0][:, 0:KT * NS].rearrange("p (k s) -> p k s", s=NS),
                           ACT.Copy).then_inc(soh, 1)

            for m in range(KT):
                residual_tile(T_XO + m, m, G_FF, 32, 17)
            norm(3, 7)

            def up(t, j, m, count):
                act.wait_ge(ps_free, t + 1)
                act.activation(tmp[:, j, :], tmp[:, j, :], ACT.Square).then_inc(link_a, 1)
                act.wait_ge(link_a, n_up0 + count + 1)
                dst = a_op[:, bass.ds(m, 1), 0, :].rearrange("p a n -> p (a n)")
                act.activation(dst, tmp[:, j, :], ACT.Copy).then_inc(h_hi, 1)

            n_up0 = n
            half = T_FF // 2
            with act.Fori(0, FG - 1) as g:
                with act.Fori(0, KT // 2) as i:
                    for j in range(2):
                        t = g * 16 + i * 2 + (T_FF + j)
                        up(t, j, i * 2 + j, g * 8 + i * 2 + j)
                        w_high(t + 2, (T_FF + j) % 2, g * 8 + i + ((T_FF + j) // 2 + 1))
                with act.Fori(0, KT // 2) as i:
                    for j in range(2):
                        t = g * 16 + i * 2 + (T_FF + KT + j)
                        w_high(t + 2, (T_FF + j) % 2, g * 8 + i + ((T_FF + KT + j) // 2 + 1))
            g = FG - 1
            with act.Fori(0, KT // 2) as i:
                for j in range(2):
                    t = i * 2 + (T_FF + 16 * g + j)
                    up(t, j, i * 2 + j, i * 2 + (g * 8 + j))
                    w_high(t + 2, (T_FF + j) % 2, i + ((T_FF + 16 * g + j) // 2 + 1))
            for m in range(KT):
                residual_tile(T_FF + 16 * g + KT + m, m, None, 0, 25)
            norm(4, 10)
            for m in range(KT):
                act.wait_ge(y_out, m + 1)
                act.dma_start(o["y"][:, m, :], x_res[:, m, :]).then_inc(out_s, 16)
            act.wait_ge(out_s, 16 * KT)

        @block.tensor
        def _(pe):
            def tile_product(t, slot, src, blocks, k_wait, ks=range(KT)):
                ps = PS[slot]
                for k in ks:
                    if k == 0 and (not isinstance(t, int) or t >= 2):
                        pe.wait_ge(ps_free, t - 1)
                    if k % (KT // 2) == 0:
                        pe.wait_ge(w_lo, t * 2 + (1 + k // (KT // 2)))
                    k_wait(k)
                    for j, (wp, xp) in enumerate(((0, 0), (0, 1), (1, 0))):
                        for b, (c0, w) in enumerate(blocks):
                            last = pe.matmul(ps[:, b, 0:w], w_split[:, slot, wp, k, :], src[:, k, xp, c0:c0 + w],
                                             start=(k == 0 and j == 0), stop=(k == KT - 1 and j == 2))
                if ks[-1] == KT - 1:
                    last.then_inc(tile_done, 1)

            ALL = [(b * CB, CB) for b in range(NB)]

            def wait_lo(n0):
                return lambda k: pe.wait_ge(op_lo, n0 + k + 1)

            def no_wait(k):
                return None

            def sums(need, n_sums, width=None):
                pe.wait_ge(acc_s, need)
                for j, (c0, w) in enumerate(ALL if width is None else [(0, width)]):
                    if j >= 2:
                        pe.wait_ge(sumr_s, n_sums + j - 1)
                    pe.matmul(M[j % 2][:, 0:w], ones[:, :], acc[:, c0:c0 + w], start=True, stop=True).then_inc(sum_s, 1)

            def fill(name, ops):
                bank, b, n = misc(name)
                if n >= 1:
                    pe.wait_ge(misc_free[b], n)
                ops(bank).then_inc(misc_full[b], 1)

            def mv_turn(g):
                def ops(bank):
                    for j in range(2):
                        for mt in range(2):
                            last = pe.transpose(bank[:, (2 * mt + j) * P:(2 * mt + j + 1) * P],
                                                mvt[:, g % 2, j, mt * P:(mt + 1) * P], ident[:, :])
                    return last
                pe.wait_ge(ps_free, PLACE["kv", 9 + 2 * g] + 1)
                fill(("mv", g), ops)

            def z_product(j):
                pair, b = divmod(j, NB)
                fill(("z", j), lambda bank: pe.matmul(bank[:, 0:CB], walpha[:, pair * P:(pair + 1) * P],
                                                      a_lr[:, b * CB:(b + 1) * CB], start=True, stop=True))

            def v_turn(m, g):
                src = r_t[:, 2 + m % 2, :]

                def ops(bank):
                    if g == 2:
                        return pe.transpose(bank[0:NS, 0:P], src[:, 0:NS], ident[:, :])
                    for j in range(4):
                        c = 4 * g + j
                        last = pe.transpose(bank[:, j * P:(j + 1) * P], src[:, NS + C * c:NS + C * (c + 1)], ident[:, :])
                    return last
                fill(("v", m, g), ops)

            def channel_sum(name, j):
                fill((name, j), lambda bank: pe.matmul(bank[:, 0:CB], ones[:, :], acc[:, j * CB:(j + 1) * CB],
                                                       start=True, stop=True))

            def unit_scores(u, g):
                l, pair, s = unit(u)

                def ops(bank):
                    for j in range(4):
                        c = 4 * g + j
                        kk = k_t[:, pair, NS + C * c:NS + C * (c + 1)] if l == 0 else tmp[:, pair, C * c:C * (c + 1)]
                        last = pe.matmul(bank[:, j * C:(j + 1) * C], kk, qz[u % 2][:, C * c:C * (c + 1)],
                                         start=True, stop=True)
                    return last
                if g == 0:
                    pe.wait_ge(lev_s, mul_count(u))
                fill(("unit", u, g), ops)

            def key_turn(g):
                def ops(bank):
                    for j in range(4):
                        c, pair = 2 * g + j // 2, j % 2
                        last = pe.transpose(bank[:, j * P:(j + 1) * P], tmp[:, pair, C * c:C * (c + 1)], ident[:, :])
                    return last
                fill(("kt", g), ops)

            pe.wait_ge(consts, 1)
            for p in range(T_OUT):
                kind, i = ORDER[p]
                if kind == "kv":
                    tile_product(p, p % 2, m_op, [(0, MEM)], wait_lo(0) if p == 0 else no_wait)
                elif p in UNITS_IN:
                    k0 = 0
                    for k, u in UNITS_IN[p] + [(KT - 1, None)]:
                        if k >= k0:
                            tile_product(p, p % 2, a_op, ALL, no_wait, range(k0, k + 1))
                        k0 = k + 1
                        if u is not None:
                            unit_scores(u, 0)
                            unit_scores(u, 1)
                else:
                    tile_product(p, p % 2, a_op, ALL, wait_lo(8) if i == 0 else no_wait)
                if p == 0:
                    sums(1, 0, MEM)
                if ("in", 0) == (kind, i):
                    sums(9, 1)
                    pe.wait_ge(sumr_s, 4)
                if p == T_OUT - 1:
                    break
                for name in AFTER.get(p, ()):
                    if name[0] == "mv":
                        mv_turn(name[1])
                    if name[0] == "z":
                        pe.wait_ge(alr_s, 1)
                        pe.wait_ge(wa_in, 16)
                        z_product(name[1])
                    if name[0] == "v":
                        pe.wait_ge(ps_free, PLACE["in", I_V + name[1]] + 1)
                        v_turn(*name[1:])
                    if name[0] == "mean":
                        pe.wait_ge(y_s, 1)
                        channel_sum(*name)
                    if name[0] == "var":
                        pe.wait_ge(lacc_s, CT)
                        channel_sum(*name)
            pe.wait_ge(qi_s, 1)
            for g in range(4):
                key_turn(g)
            def chunk_sum(c):
                if c % 2 == 0:
                    wait_read(pe, ("kt", c // 2))
                if c >= 2:
                    pe.wait_ge(st_s, 4 * (c - 1))
                for pair in range(2):
                    last = pe.matmul(PS[0][:, c % 2, pair * 256:(pair + 1) * 256], k_in[:, c, pair, :],
                                     v_tok[:, c, pair * 256:(pair + 1) * 256], start=True, stop=True)
                last.then_inc(kvp_s, 1)

            def outputs(r):
                if r >= 1:
                    pe.wait_ge(st_s, 4 * (2 * r + 1))
                if r >= 2:
                    pe.wait_ge(gor_s, r - 1)
                    pe.wait_ge(goo_s, r - 1)
                for j in range(4):
                    c, pair = 2 * r + j // 2, j % 2
                    if r == 0 and c == 1:
                        pe.wait_ge(st_s, 4)
                    for par_ in range(2):
                        h, p0 = 2 * pair + par_, DK * par_
                        dst = go_bank[r % 2][par_][:, j * C:(j + 1) * C]
                        last = pe.matmul(dst, v_tok[:, c, h * DV:(h + 1) * DV], sc_t[:, pair, c, par_, :], start=True, stop=(c == 0))
                        if c >= 1:
                            last = pe.matmul(dst, state[p0:p0 + DK, c - 1, pair, :],
                                             q_t[p0:p0 + DK, pair, NS + C * c:NS + C * (c + 1)], start=False, stop=True)
                last.then_inc(go_s, 1)

            pe.wait_ge(ps_free, T_OUT)
            for g in range(2):
                wait_read(pe, ("unit", N_UNITS - 1, g))
            for c in range(4):
                chunk_sum(c)
            pe.wait_ge(qi_s, 2)
            for r in range(NR):
                outputs(r)
                for c in (2 * r + 4, 2 * r + 5):
                    if c < NC_:
                        chunk_sum(c)

            def wait_conv(k):
                pe.wait_ge(conv_lo, k + 1)

            pe.wait_ge(gor_s, NR)
            pe.wait_ge(goo_s, NR)
            tile_product(T_OUT, T_OUT % 2, a_op, ALL, wait_conv, range(0, CT))
            pe.wait_ge(stn_s, 2)
            pe.wait_ge(smp_s, 1)

            def sample_out(bank):
                for pair in range(2):
                    for s in range(NS):
                        j = pair * NS + s
                        last = pe.matmul(bank[:, 2 * j:2 * j + 2], st_smp[:, pair, s * DV:(s + 1) * DV],
                                         small[:, 80 + 2 * j:82 + 2 * j], start=True, stop=True)
                return last
            fill(("smp", 0), sample_out)
            pe.wait_ge(gsq_s, 2 * NR + H)
            pe.wait_ge(osr_s, 1)
            for n_ in range(H * NB):
                h, j = divmod(n_, NB)
                if n_ >= 2:
                    pe.wait_ge(gnr_s, n_ - 1)
                pe.matmul(M[n_ % 2][:, 0:CB], ones[:, :], sq_t[:, h, j * CB:(j + 1) * CB], start=True, stop=True).then_inc(gn_s, 1)

            def wait_gla(k):
                pe.wait_ge(gla_lo, k - CT + 1)

            tile_product(T_OUT + 1, (T_OUT + 1) % 2, a_op, ALL, no_wait, range(0, CT))
            for t in (T_OUT, T_OUT + 1):
                tile_product(t, t % 2, a_op, ALL, wait_gla, range(CT, KT))
            for m in range(2, KT):
                t = T_OUT + m
                tile_product(t, t % 2, a_op, ALL, no_wait)

            def q_tiles(h):
                for j in range(2):
                    t = T_XQ + 2 * h + j
                    tile_product(t, t % 2, b_op, ALL, wait_lo(16) if t == T_XQ else no_wait)
                    if t == T_XQ:
                        sums(17, 4)

            q_tiles(0)
            for h in range(H):
                pe.wait_ge(kv_lo, h + 1)
                pe.wait_ge(q_lo, 2 * h + 2)
                if h == 0:
                    pe.wait_ge(sumr_s, 7)
                for c in range(NC_):
                    if c >= 2:
                        pe.wait_ge(e_s, NC_ * h + c - 1)
                    elif h >= 1:
                        pe.wait_ge(ol_s, 4 * h)
                    c0 = NS + C * c
                    for k in range(2):
                        for j, (qp, kp) in enumerate(((0, 0), (0, 1), (1, 0))):
                            last = pe.matmul(M[c % 2][:, 0:MEM], a_op[:, 2 * h + k, qp, c0:c0 + C], kv[:, h % 2, kp, k, :],
                                             start=(k == 0 and j == 0), stop=(k == 1 and j == 2))
                    last.then_inc(qk_s, 1)
                if h + 1 < H:
                    q_tiles(h + 1)
                t_last = T_XQ + 2 * min(h + 1, H - 1) + 1
                pe.wait_ge(ps_free, t_last + 1)
                for u in range(2):
                    pe.wait_ge(p_s, NC_ * h + 4 * (u + 1))
                    for mt in range(2):
                        for j in range(4):
                            last = pe.transpose(PS[u][:, mt, j * C:(j + 1) * C],
                                                ex[:, 4 * u + j, mt * P:(mt + 1) * P], ident[:, :])
                    last.then_inc(ptd, 1)
                for u in range(2):
                    pe.wait_ge(pt_lo, 2 * h + u + 1)
                    for d in range(2):
                        dst = PS[u][:, 2, :] if d == 0 else M[u][:, :]
                        for mt in range(2):
                            for j, (vp, pp) in enumerate(((0, 0), (0, 1), (1, 0))):
                                last = pe.matmul(dst, kv[:, h % 2, vp, 2 + mt, d * P:(d + 1) * P], pt[:, mt, pp, :],
                                                 start=(mt == 0 and j == 0), stop=(mt == 1 and j == 2))
                        last.then_inc(pv_s, 1)
            pe.wait_ge(qz_s, 1)
            pe.wait_ge(ol_s, 16)
            for s in range(NS):
                pe.wait_ge(ca[s % NCS], 16 * (s // NCS + 1))
                for k in range(KT):
                    r = H * s + k // 2
                    p0 = 32 + 32 * s - r
                    last = pe.matmul(M[0][0:32, 0:MEM], qzs[:, k, p0:p0 + 32], cache[s % NCS][:, k * MEM:(k + 1) * MEM],
                                     start=(s == 0 and k == 0), stop=(s == NS - 1 and k == KT - 1))
                last.then_inc(cu, 1)
            pe.wait_ge(sp_s, 1)
            for mt in range(2):
                last = pe.transpose(M[1][:, mt * 32:(mt + 1) * 32], ex[0:32, 0, mt * P:(mt + 1) * P], ident[0:32, 0:32])
            last.then_inc(spt, 1)
            pe.wait_ge(pz_s, 3)
            for s in range(NS):
                r = NS + s
                pe.wait_ge(ca[r % NCS], 16 * (r // NCS + 1))
                for h in range(H):
                    dst = PS[0][0:NS, h, 0:HD] if h < 3 else PS[1][0:NS, 0, 0:HD]
                    for mt in range(2):
                        last = pe.matmul(dst, pz[:, mt, h, 8 + 7 * s:16 + 7 * s],
                                         cache[r % NCS][:, mt * D + h * HD:mt * D + (h + 1) * HD],
                                         start=(s == 0 and mt == 0), stop=(s == NS - 1 and mt == 1))
                last.then_inc(cu, 1)
            pe.wait_ge(sor_s, 2)
            for k in range(KT):
                last = pe.transpose(M[0][:, k * NS:(k + 1) * NS], o_smp[:, k * P:(k + 1) * P], ident[0:NS, 0:NS])
            last.then_inc(sot, 1)

            pe.wait_ge(sol, 1)
            for m in range(KT):
                t = T_XO + m
                tile_product(t, t % 2, a_op, ALL, no_wait)

            def last_two(sem_, n0):
                def wait(k):
                    if k == 0:
                        pe.wait_ge(sem_, n0 + (KT - 1))
                    if k == KT - 1:
                        pe.wait_ge(sem_, n0 + KT)
                return wait

            def ffn_group(g, first=False, rest=0):
                with pe.Fori(1 if first else 0, KT // 2) as i:
                    for j in range(2):
                        tile_product(g * 16 + i * 2 + (T_FF + j), (T_FF + j) % 2, b_op, ALL, no_wait)
                with pe.Fori(0, KT // 2) as i:
                    for j in range(2):
                        tile_product(g * 16 + i * 2 + (T_FF + KT + j), (T_FF + j) % 2, a_op, ALL,
                                     last_two(h_lo, g * 8))

            tile_product(T_FF, T_FF % 2, b_op, ALL, wait_lo(24))
            sums(25, 7)
            tile_product(T_FF + 1, (T_FF + 1) % 2, b_op, ALL, no_wait)
            ffn_group(0, first=True)
            with pe.Fori(1, FG) as g:
                ffn_group(g)
            sums(33, 10)

        @block.vector
        def _(dve):
            n = 0

            def link(ins):
                nonlocal n
                n += 1
                ins.then_inc(link_v, 1)
                dve.wait_ge(link_v, n)

            dve.memset(small[:, 128:129], EPS).then_inc(eps_s, 1)

            def low(dst, src, gain, hi, sem_, need):
                dve.wait_ge(sem_, need)
                if gain is None:
                    return dve.tensor_tensor(dst, src, hi.bitcast(F32), ALU.subtract)
                return dve.scalar_tensor_tensor(out=dst, in0=src, scalar=gain, in1=hi.bitcast(F32),
                                                op0=ALU.mult, op1=ALU.subtract)

            for k in range(KT):
                low(m_op[:, k, 1, :], m_raw[:, k, :], par[:, G_MEM + k:G_MEM + k + 1], m_op[:, k, 0, :],
                    op_hi, k + 1).then_inc(op_lo, 1)
            dve.wait_ge(sq_s, 1)
            dve.tensor_reduce(acc[:, 0:MEM], msq[:, :, :].rearrange("p k n -> p n k"), AX, ALU.add).then_inc(acc_s, 1)

            def kv_evac(n):
                p = PLACE["kv", n]
                dve.wait_ge(tile_done, p + 1)
                if n == 0:
                    dve.wait_ge(rstd_s, 1)
                g = n // 2
                if n < 8:
                    dst = m_out[:, g % 2, n % 2, :]
                    if g >= 2 and n % 2 == 0:
                        dve.wait_ge(kvst, 16 * (g - 1))
                else:
                    dst = mvt[:, g % 2, n % 2, :]
                    if g >= 6 and n % 2 == 0:
                        wait_full(dve, ("mv", g - 6))
                dve.tensor_tensor(dst, PS[p % 2][:, 0, 0:MEM], m_rstd[:, :], ALU.mult).then_inc(ps_free, 1)

            for k in range(KT):
                low(a_op[:, k, 1, :], x_in[:, k, :], par[:, G_MIX + k:G_MIX + k + 1], a_op[:, k, 0, :],
                    op_hi, 8 + k + 1).then_inc(op_lo, 1)
                if k % 2 == 0:
                    kv_evac(k // 2)
            for k in range(KT):
                dve.wait_ge(sq_s, 1 + k + 1)
                if k == 0:
                    dve.engine_nop().then_inc(acc_s, 1)
                else:
                    dve.wait_ge(acc_s, 1 + k)
                    dve.tensor_tensor(acc[:, :], acc[:, :], tmp[:, k % 2, :], ALU.add).then_inc(acc_s, 1)

            def tap(j):
                m, w = TAPS_DVE[j]
                dst = conv_y[:, m, NS:T]
                src = conv_in[:, m, w:w + SEQ]
                t_ = par[:, P_WDW + m * CW + w:P_WDW + m * CW + w + 1]
                if w == 0:
                    link(dve.tensor_scalar(dst, src, t_, par[:, P_BDW + m:P_BDW + m + 1], ALU.mult, ALU.add))
                else:
                    link(dve.scalar_tensor_tensor(out=dst, in0=src, scalar=t_, in1=dst, op0=ALU.mult, op1=ALU.add))

            def level_mul(u):
                l, pair, s = unit(u)
                q4 = q_t[:, pair, NS:T]
                if u >= 2:
                    wait_full(dve, ("unit", u - 2, 1))
                    dve.wait_ge(lexp_s, u - 1)
                    lv = tmp[:, pair, 0:SEQ]
                    if s == 1:
                        dve.tensor_tensor(lv, lv, k_t[:, pair, NS:T], ALU.mult).then_inc(lev_s, 1)
                    else:
                        ee, eo = even_odd(lv, s)
                        dve.tensor_tensor(ee, ee, even_odd(k_t[:, pair, NS:T], s)[0], ALU.mult).then_inc(lev_s, 1)
                for par_ in range(2):
                    rows = slice(DK * par_, DK * (par_ + 1))
                    s_ = max(s, 1)
                    dst = qz[u % 2][rows, :].rearrange("p (c a n s) -> p c a n s", c=NC_, a=2, s=s_)[:, :, par_, :, :]
                    qe, qo = (v.rearrange("p (c n) s -> p c n s", c=NC_) for v in even_odd(q4[rows, :], s_))
                    if l <= 1:
                        dve.tensor_copy(dst, qe if l == 0 else qo).then_inc(lev_s, 1)
                    else:
                        eo = even_odd(tmp[rows, pair, 0:SEQ], s)[1].rearrange("p (c n) s -> p c n s", c=NC_)
                        dve.tensor_tensor(dst, eo, qo, ALU.mult).then_inc(lev_s, 1)

            def level_select(u, g):
                l, pair, s = unit(u)
                bank, b, _ = misc(("unit", u, g))
                s_ = max(s, 1)
                wait_full(dve, ("unit", u, g))
                dst = sc_t[:, pair, 4 * g:4 * g + 4, :, :].rearrange("p c a (n e s) -> p (c a) n e s", e=2, s=s_)
                e = 0 if l == 0 else 1
                mk = even_odd(mask[:, l, :], s_)[e].unsqueeze(1).broadcast_to([P, 8, C // (2 * s_), s_])
                dve.copy_predicated(dst[:, :, :, e, :], mk, bank[:, :].rearrange("p (x n s) -> p x n s", x=8, s=s_)).then_inc(misc_free[b], 1)

            for p in range(4, T_OUT):
                kind, i = ORDER[p]
                for _, u in UNITS_IN.get(p, ()):
                    if u == 0:
                        dve.wait_ge(zero_s, 1)
                    level_select(u, 0)
                    if u + 1 < N_UNITS:
                        level_mul(u + 1)
                    level_select(u, 1)
                if p == T_OUT - 1:
                    b4 = prompt(la).rearrange("p a (c n) -> p a c n", n=C)
                    endb = b4[:, :, :, C - 1:C].broadcast_to([P, 2, NC_, C])
                    kx = tmp[:, :, 0:SEQ]
                    dve.tensor_tensor(kx.rearrange("p a (c n) -> p a c n", n=C), endb, b4, ALU.subtract).then_inc(kx_s, 1)
                    dve.wait_ge(kx_s2, 1)
                    dve.tensor_tensor(kx, kx, prompt(k_t), ALU.mult).then_inc(qi_s, 1)
                    dve.wait_ge(kx_s2, 2)
                    dve.tensor_tensor(prompt(q_t), prompt(q_t), prompt(la), ALU.mult).then_inc(qi_s, 1)
                    dve.wait_ge(qi_s, 2)
                if kind == "kv":
                    kv_evac(i)
                else:
                    dve.wait_ge(tile_done, p + 1)
                    if i == 0:
                        dve.wait_ge(rstd_s, 2)
                        link(dve.memset(conv_in[:, :, 0:CW - 1], 0.0))
                    ps = pcols(p % 2)
                    if i < 8:
                        m, gate = divmod(i, 2)
                        dve.tensor_tensor(cols(tmp[:, gate, :]), ps, cols(rstd[:, :]), ALU.mult).then_inc(ps_free, 1)
                        if gate:
                            dve.wait_ge(sig_s, m + 1)
                            if m == 0:
                                dve.wait_ge(cs_in, 16)
                            dve.tensor_tensor(conv_in[:, m, CW - 1:], tmp[:, 0, NS:T], tmp[:, 1, NS:T], ALU.mult).then_inc(u_s, 1)
                            dve.tensor_tensor(conv_smp[:, m, :, CW - 1], tmp[:, 0, 0:NS], tmp[:, 1, 0:NS], ALU.mult).then_inc(u_s, 1)
                            dve.wait_ge(u_s, 2 * m + 2)
                    elif i == I_A:
                        dve.tensor_tensor(cols(a_lr[:, :]), PS[p % 2][0:RANK, :, 0:CB], cols(rstd[0:RANK, :]),
                                          ALU.mult).then_inc(ps_free, 1)
                        dve.wait_ge(ps_free, p + 1)
                        dve.engine_nop().then_inc(alr_s, 1)
                    elif i < I_Q:
                        dve.tensor_tensor(cols(k_t[:, i - I_K, :]), ps, cols(rstd[:, :]), ALU.mult).then_inc(ps_free, 1)
                    elif i < I_V:
                        dve.scalar_tensor_tensor(out=cols(q_t[:, i - I_Q, :]), in0=ps, scalar=DK ** -0.5, in1=cols(rstd[:, :]),
                                                 op0=ALU.mult, op1=ALU.mult).then_inc(ps_free, 1)
                    elif i < I_R:
                        m = i - I_V
                        if m == 0:
                            wait_full(dve, ("mv", 3))
                        if m == 1:
                            dve.wait_ge(kvst, 128)
                        if m >= 2:
                            wait_full(dve, ("v", m - 2, 2))
                        dve.tensor_tensor(cols(r_t[:, 2 + m % 2, :]), ps, cols(rstd[:, :]), ALU.mult).then_inc(ps_free, 1)
                    else:
                        if i == I_R:
                            dve.wait_ge(pool_tap, CW)
                        if i >= I_R + 2:
                            wait_full(dve, ("v", 3, 2))
                        dve.tensor_tensor(cols(r_t[:, i - I_R, :]), ps, cols(rstd[:, :]), ALU.mult).then_inc(ps_free, 1)
                for j in range(*taps_after(p)[0]):
                    tap(j)
                if kind == "in" and i == 7:
                    for m in range(CT):
                        wd = par[:, P_WDW + m * CW:P_WDW + (m + 1) * CW].unsqueeze(1).broadcast_to([P, NS, CW])
                        pr = tmp[:, 0, 0:NS * CW].rearrange("p (s w) -> p s w", s=NS)
                        link(dve.tensor_tensor(pr, conv_smp[:, m, :, :], wd, ALU.mult))
                        link(dve.tensor_reduce(conv_y[:, m, 0:NS], pr, AX, ALU.add))
                        link(dve.tensor_scalar(conv_y[:, m, 0:NS], conv_y[:, m, 0:NS], par[:, P_BDW + m:P_BDW + m + 1], None, ALU.add))
                if kind == "in" and i == I_K:
                    for j in range(2 * NB):
                        pair, b = divmod(j, NB)
                        bank, bk, _ = misc(("z", j))
                        wait_full(dve, ("z", j))
                        dve.tensor_scalar(la[:, pair, b * CB:(b + 1) * CB], bank[:, 0:CB],
                                          par[:, P_BAL + pair:P_BAL + pair + 1], None, ALU.add).then_inc(misc_free[bk], 1)
                if kind == "in" and i == I_Q:
                    dve.wait_ge(soft_s, 1)
                    link(dve.scalar_tensor_tensor(out=la[:, :, :], in0=la[:, :, :], scalar=0.0, in1=lnz,
                                                  op0=ALU.min, op1=ALU.subtract))
                    for pair in range(2):
                        z = la[:, pair, NS:T]
                        link(dve.tensor_tensor_scan(z, keep[:, :], z, 0.0, ALU.mult, ALU.add))
                if kind == "in" and i == I_V:
                    link(dve.tensor_copy(small[:, 64:80].rearrange("p (a s) -> p a s", a=2), k_t[:, :, 0:NS]))
                    link(dve.memset(small[:, 80:112], 0.0))
                    for par_ in range(2):
                        rows = slice(DK * par_, DK * (par_ + 1))
                        dst = small[rows, 80:112].rearrange("p (a s b) -> p a s b", a=2, b=2)[:, :, :, par_]
                        link(dve.tensor_copy(dst, q_t[rows, :, 0:NS]))
                    dve.engine_nop().then_inc(smp_s, 1)
                    dve.engine_nop().then_inc(dve_tap, 1)
                if kind == "in" and i == I_V:
                    dve.wait_ge(pool_tap, CW)
                    link(dve.tensor_tensor(acc[:, :], conv_y[:, 0, :], conv_y[:, 1, :], ALU.add))
                    link(dve.tensor_tensor(acc[:, :], acc[:, :], conv_y[:, 2, :], ALU.add))
                    dve.tensor_tensor(acc[:, :], acc[:, :], conv_y[:, 3, :], ALU.add).then_inc(y_s, 1)
                if kind == "in" and i == I_V + 1:
                    for b in range(NB):
                        wait_read(dve, ("mean", b))
                    for m in range(CT):
                        dve.tensor_tensor(conv_y[:, m, :], conv_y[:, m, :], tmp[:, 0, :], ALU.subtract).then_inc(mean_s, 1)
                    for m in range(CT):
                        dve.wait_ge(lsq_s, m + 1)
                        if m == 0:
                            dve.engine_nop().then_inc(lacc_s, 1)
                        else:
                            dve.wait_ge(lacc_s, m)
                            dve.tensor_tensor(acc[:, :], acc[:, :], tmp[:, 1, :], ALU.add).then_inc(lacc_s, 1)
                if kind == "in" and i == I_V + 2:
                    dve.wait_ge(lnr_s, 1)
                    for m in range(CT):
                        dve.tensor_tensor(conv_y[:, m, :], conv_y[:, m, :], tmp[:, 0, :], ALU.mult).then_inc(yn_s, 1)
                    dve.wait_ge(conv_st, 32)
                    for u in range(2):
                        link(dve.memset(qz[u][:, :], 0.0) if u else dve.memset(qz[0], 0.0))
                    level_mul(0)
            def state_after(c):
                dve.wait_ge(kvp_s, c + 1)
                for h in range(H):
                    p0, pair = DK * (h % 2), h // 2
                    kvp = PS[0][p0:p0 + DK, c % 2, h * DV:(h + 1) * DV]
                    if c == 0:
                        dve.tensor_copy(state[p0:p0 + DK, 0, pair, :], kvp).then_inc(st_s, 1)
                    else:
                        if h == 0:
                            dve.wait_ge(st_s, H * c)
                            dve.wait_ge(dec_s, 1)
                        dve.scalar_tensor_tensor(out=state[p0:p0 + DK, c, pair, :], in0=state[p0:p0 + DK, c - 1, pair, :],
                                                 scalar=small[p0:p0 + DK, pair * NC_ + c:pair * NC_ + c + 1], in1=kvp,
                                                 op0=ALU.mult, op1=ALU.add).then_inc(st_s, 1)

            for c in range(4):
                state_after(c)
            for r in range(NR):
                dve.wait_ge(go_s, r + 1)
                dve.tensor_copy(sc_t[:, :, 2 * r:2 * r + 2, 0, :], go_bank[r % 2][0][:, :].rearrange(
                    "p (c a n) -> p a c n", c=2, a=2)).then_inc(gor_s, 1)
                for c in (2 * r + 4, 2 * r + 5):
                    if c < NC_:
                        state_after(c)
            bank, b, _ = misc(("smp", 0))
            wait_full(dve, ("smp", 0))
            dve.tensor_copy(small[:, 160:192], bank[:, 0:32]).then_inc(osr_s, 1)
            for h in range(H + 1):
                if h < H:
                    dve.wait_ge(grs_s, h + 1)
                    dve.wait_ge(osr_s, 1)
                    s3 = sq_t[:, h, NS:T].rearrange("p (c n) -> p c n", n=C)
                    dve.tensor_tensor(s3, s3, sc_t[:, h // 2, :, h % 2, :], ALU.mult).then_inc(gm_s, 1)
                    dve.tensor_tensor(sq_t[:, h, 0:NS], sq_t[:, h, 0:NS], o_cols(h), ALU.mult).then_inc(gm_s, 1)
                    dve.wait_ge(silu_s, h + 1)
                    dve.wait_ge(gm_s, 3 * h + 2)
                    dve.scalar_tensor_tensor(out=sq_t[:, h, :], in0=sq_t[:, h, :], scalar=par[:, P_GLAG:P_GLAG + 1],
                                             in1=r_t[:, h, :], op0=ALU.mult, op1=ALU.mult).then_inc(gm_s, 1)
                if h >= 1:
                    if h == 3:
                        dve.wait_ge(gla_lo, 2)
                    low(a_op[:, CT + h - 1, 1, :], sq_t[:, h - 1, :], None, a_op[:, CT + h - 1, 0, :], op_hi, 20 + h).then_inc(gla_lo, 1)

            def residual_tile(t, m, gain, n_op, n_sq):
                dve.wait_ge(tile_done, t + 1)
                dve.tensor_tensor(cols(x_res[:, m, :]), cols(x_res[:, m, :]), pcols(t % 2), ALU.add).then_inc(ps_free, 1)
                if gain is not None:
                    low(b_op[:, m, 1, :], x_res[:, m, :], par[:, gain + m:gain + m + 1], b_op[:, m, 0, :],
                        op_hi, n_op + m + 1).then_inc(op_lo, 1)
                dve.wait_ge(sq_s, n_sq + m + 1)
                if m == 0:
                    dve.engine_nop().then_inc(acc_s, 1)
                else:
                    dve.wait_ge(acc_s, n_sq + m)
                    dve.tensor_tensor(acc[:, :], acc[:, :], tmp[:, m % 2, :], ALU.add).then_inc(acc_s, 1)

            for m in range(KT):
                if m in (0, 2):
                    dve.wait_ge(xr[m // 2], 16)
                residual_tile(T_OUT + m, m, G_XA, 24, 9)

            def kv_low(h):
                dve.wait_ge(kv_hi, h + 1)
                dve.tensor_tensor(kv[:, h % 2, 1, :, :], kv_raw[:, :, :], kv[:, h % 2, 0, :, :].bitcast(F32),
                                  ALU.subtract).then_inc(kv_lo, 1)

            def q_tiles(h):
                for j in range(2):
                    t = T_XQ + 2 * h + j
                    dve.wait_ge(tile_done, t + 1)
                    if t == T_XQ:
                        dve.wait_ge(rstd_s, 3)
                    if h >= 1:
                        dve.wait_ge(q_lo, 2 * h)
                    dve.tensor_tensor(cols(tmp[:, j, :]), pcols(t % 2), cols(rstd[:, :]), ALU.mult).then_inc(ps_free, 1)
                    low(a_op[:, 2 * h + j, 1, :], tmp[:, j, :], None, a_op[:, 2 * h + j, 0, :], q_hi, 2 * h + j + 1).then_inc(q_lo, 1)
                    link(dve.tensor_copy(small[:, 64 + 8 * (2 * h + j):72 + 8 * (2 * h + j)], tmp[:, j, 0:NS]))

            q_tiles(0)
            kv_low(0)
            for h in range(H):
                def chunk_scale(c):
                    dve.wait_ge(e_s, NC_ * h + c + 1)
                    link(dve.reciprocal(small[:, 40 + c:41 + c], small[:, 40 + c:41 + c]))
                    dve.tensor_scalar(ex[:, c, :], ex[:, c, :], small[:, 40 + c:41 + c], None, ALU.mult).then_inc(p_s, 1)

                for c in range(NC_):
                    dve.wait_ge(qk_s, NC_ * h + c + 1)
                    link(dve.tensor_reduce(small[:, 32 + c:33 + c], M[c % 2][:, 0:MEM], AX, ALU.max))
                    dve.tensor_scalar(small[:, 32 + c:33 + c], small[:, 32 + c:33 + c], -(HD ** -0.5), None,
                                      ALU.mult).then_inc(nm_s, 1)
                    if c >= 1:
                        chunk_scale(c - 1)
                chunk_scale(NC_ - 1)
                if h + 1 < H:
                    kv_low(h + 1)
                    q_tiles(h + 1)
                for u in range(2):
                    dve.wait_ge(pt_hi, 2 * h + u + 1)
                    dve.tensor_tensor(pt[:, :, 1, :], PS[u][:, 0:2, :], pt[:, :, 0, :].bitcast(F32),
                                      ALU.subtract).then_inc(pt_lo, 1)
                for u in range(2):
                    for d in range(2):
                        dve.wait_ge(oh_s, 4 * h + 2 * u + d + 1)
                        src = PS[u][:, 2, :] if d == 0 else M[u][:, :]
                        c0 = NS + 512 * u
                        dve.tensor_tensor(a_op[:, 2 * h + d, 1, c0:c0 + 512], src,
                                          a_op[:, 2 * h + d, 0, c0:c0 + 512].bitcast(F32), ALU.subtract).then_inc(ol_s, 1)
            dve.wait_ge(tile_done, T_XO)
            link(dve.memset(qzs[:, :, :], 0.0))
            dve.memset(pz[:, :, :, :], 0.0).then_inc(pz_s, 1)
            qd = qzs[:, :, 32:288].rearrange("p k (s n) -> p k s n", n=32)[:, :, :, 0]
            dve.tensor_copy(qd, small[:, 64:128].rearrange("p (k s) -> p k s", s=NS)).then_inc(qz_s, 1)
            dve.wait_ge(cu, NS)
            link(dve.tensor_reduce(small[0:32, 32:33], M[0][0:32, 0:MEM], AX, ALU.max))
            dve.tensor_scalar(small[0:32, 32:33], small[0:32, 32:33], -(HD ** -0.5), None, ALU.mult).then_inc(sm_s, 1)
            dve.wait_ge(se_s, 1)
            link(dve.reciprocal(small[0:32, 40:41], small[0:32, 40:41]))
            dve.tensor_scalar(ex[0:32, 0, :], ex[0:32, 0, :], small[0:32, 40:41], None, ALU.mult).then_inc(sp_s, 1)
            dve.wait_ge(spt, 1)
            for mt in range(2):
                dst = pz[:, mt, :, 8:72].rearrange("p h (s n) -> p h s n", n=8)[:, :, :, 0]
                dve.tensor_copy(dst, M[1][:, mt * 32:(mt + 1) * 32].rearrange("p (s h) -> p h s", h=H)).then_inc(pz_s, 1)
            dve.wait_ge(cu, 2 * NS)
            dve.tensor_copy(o_smp[:, 0:3 * HD].rearrange("p (h n) -> p h n", h=3), PS[0][0:NS, :, 0:HD]).then_inc(sor_s, 1)
            dve.tensor_copy(o_smp[:, 3 * HD:], PS[1][0:NS, 0, 0:HD]).then_inc(sor_s, 1)
            dve.wait_ge(soh, 1)
            dve.tensor_tensor(a_op[:, :, 1, 0:NS], M[0][:, 0:KT * NS].rearrange("p (k s) -> p k s", s=NS),
                              a_op[:, :, 0, 0:NS].bitcast(F32), ALU.subtract).then_inc(sol, 1)

            dve.wait_ge(xld, 16)
            for m in range(KT):
                residual_tile(T_XO + m, m, G_FF, 32, 17)

            def up(t, j, m, count):
                dve.wait_ge(tile_done, t + 1)
                dve.scalar_tensor_tensor(out=cols(tmp[:, j, :]), in0=pcols((T_FF + j) % 2), scalar=0.0,
                                         in1=cols(rstd[:, :]), op0=ALU.max, op1=ALU.mult).then_inc(ps_free, 1)
                dve.wait_ge(h_hi, count + 1)
                hi = a_op[:, bass.ds(m, 1), 0, :].rearrange("p a n -> p (a n)").bitcast(F32)
                dst = a_op[:, bass.ds(m, 1), 1, :].rearrange("p a n -> p (a n)")
                dve.tensor_tensor(dst, tmp[:, j, :], hi, ALU.subtract).then_inc(h_lo, 1)

            def down(t, j, m):
                dve.wait_ge(tile_done, t + 1)
                x = x_res[:, bass.ds(m, 1), :].rearrange("p a (b c) -> p (a b) c", b=NB)
                dve.tensor_tensor(x, x, pcols((T_FF + j) % 2), ALU.add).then_inc(ps_free, 1)

            dve.wait_ge(rstd_s, 4)
            dve.wait_ge(acc_s, 25)
            with dve.Fori(0, FG - 1) as g:
                with dve.Fori(0, KT // 2) as i:
                    for j in range(2):
                        up(g * 16 + i * 2 + (T_FF + j), j, i * 2 + j, g * 8 + i * 2 + (j + 0))
                with dve.Fori(0, KT // 2) as i:
                    for j in range(2):
                        down(g * 16 + i * 2 + (T_FF + KT + j), j, i * 2 + j)
            g = FG - 1
            with dve.Fori(0, KT // 2) as i:
                for j in range(2):
                    up(i * 2 + (T_FF + 16 * g + j), j, i * 2 + j, i * 2 + (g * 8 + j))
            for m in range(KT):
                residual_tile(T_FF + 16 * g + KT + m, m, None, 0, 25)
            dve.wait_ge(rstd_s, 5)
            for m in range(KT):
                dve.scalar_tensor_tensor(out=x_res[:, m, :], in0=x_res[:, m, :], scalar=par[:, G_FIN + m:G_FIN + m + 1],
                                         in1=rstd[:, :], op0=ALU.mult, op1=ALU.mult).then_inc(y_out, 1)


def kernel(x_prompt, x_sample, cache_conv, state_gla, cache_mem_k, cache_mem_v, mem_prompt, norm_mix_g, w_in,
           w_alpha, b_alpha, w_dw, b_dw, conv_ln_g, conv_ln_b, gla_norm_g, w_out, norm_xa_g, mem_norm_g, w_xq,
           w_xk, w_xv, w_xo, norm_ffn_g, w_up, w_down, final_g):
    import numpy as np
    import concourse.bacc as bacc
    from concourse.bass_utils import run_bass_kernel_spmd as run

    f32 = np.float32

    def tiles(w):
        w = np.asarray(w)
        k, n = w.shape
        return w.reshape(k // D, KT, P, n // P, P).transpose(3, 0, 2, 1, 4)

    def feat(v):
        return np.asarray(v).reshape(-1, P).T

    w = np.asarray(w_in)[0]
    cv, cg, qq, kk, vv, rr, aa = np.split(w, [512, 1024, 1280, 1536, 2048, 2560], axis=1)
    conv = np.stack([cv.reshape(D, CT, P), cg.reshape(D, CT, P)], axis=2).reshape(D, 2 * DC)
    a_pad = np.concatenate([aa, np.zeros((D, P - RANK), f32)], axis=1)
    w_in_r = np.concatenate([conv, a_pad, kk, qq, vv, rr], axis=1)
    parts = [tiles(m)[:, 0] for m in (w_xk[0], w_xv[0], w_in_r, w_out[0], w_xq[0], w_xo[0])]
    up, down = tiles(w_up[0])[:, 0], tiles(w_down[0])
    for g in range(FG):
        parts += [up[g * KT:(g + 1) * KT], down[:, g]]
    wt = np.concatenate(parts, axis=0)
    order = [n if kind == "kv" else T_IN + n for kind, n in ORDER]
    wt = np.concatenate([wt[order], wt[T_OUT:]], axis=0)

    x = np.concatenate([np.asarray(x_sample)[:, 0], np.asarray(x_prompt)[0]], axis=0)
    wdw = np.asarray(w_dw)[0].T.reshape(CT, P, CW).transpose(1, 0, 2).reshape(P, CT * CW)
    par = np.concatenate([feat(mem_norm_g[0]), feat(norm_mix_g[0]), feat(norm_xa_g[0]), feat(norm_ffn_g[0]),
                          feat(final_g), feat(b_dw[0]), feat(conv_ln_g[0]), feat(conv_ln_b[0]),
                          feat(gla_norm_g[0]), feat(b_alpha[0]), wdw], axis=1)
    cc = np.asarray(cache_conv)[0].reshape(NS, CW - 1, CT, P).transpose(3, 2, 0, 1)
    cc = np.concatenate([cc, np.zeros((P, CT, NS, 1), f32)], axis=3)
    arrays = {
        "wt": wt,
        "x": x.T.reshape(KT, P, T).transpose(1, 0, 2),
        "mem": np.asarray(mem_prompt)[0].T.reshape(KT, P, MEM).transpose(1, 0, 2),
        "par": par,
        "w_alpha": np.asarray(w_alpha)[0],
        "conv_cache": cc,
        "state": np.asarray(state_gla)[0].reshape(NS, 2, 2, DK, DV).transpose(2, 3, 1, 0, 4).reshape(P, 2, NS, DV),
        "cache_k": np.asarray(cache_mem_k)[0].reshape(NS, MEM, KT, P).transpose(0, 3, 2, 1).reshape(NS, P, KT * MEM),
        "cache_v": np.asarray(cache_mem_v)[0].reshape(NS, 2, P, D).transpose(0, 2, 1, 3).reshape(NS, P, 2 * D),
    }
    outs = {"y": (P, KT, T), "mk": (P, KT, MEM), "mv": (P, 2, D), "conv_p": (P, CT, CW - 1),
            "conv_s": (P, CT, NS, CW - 1), "gla_p": (P, 2, DV), "gla_s": (P, 2, NS, DV)}

    nc = bacc.Bacc("TRN2", target_bir_lowering=False, num_devices=1)
    arrays = {k: np.ascontiguousarray(v) for k, v in arrays.items()}
    ins = {k: nc.dram_tensor(f"in_{k}", v.shape, F32, kind="ExternalInput").ap() for k, v in arrays.items()}
    out = {k: nc.dram_tensor(f"out_{k}", v, F32, kind="ExternalOutput").ap() for k, v in outs.items()}
    build(nc, ins, out)
    r = run(nc, [{f"in_{k}": v for k, v in arrays.items()}], core_ids=[0]).results[0]
    r = {k: np.asarray(r[f"out_{k}"]) for k in outs}

    y = r["y"].transpose(2, 1, 0).reshape(T, D)
    return (y[NS:].reshape(1, SEQ, D), y[:NS].reshape(NS, 1, D),
            r["conv_p"].transpose(2, 1, 0).reshape(1, 1, CW - 1, DC),
            r["conv_s"].transpose(2, 3, 1, 0).reshape(1, NS, CW - 1, DC),
            r["gla_p"].reshape(2, DK, 2, DV).transpose(2, 0, 1, 3).reshape(1, 1, H, DK, DV),
            r["gla_s"].reshape(2, DK, 2, NS, DV).transpose(3, 2, 0, 1, 4).reshape(1, NS, H, DK, DV),
            r["mk"].transpose(2, 1, 0).reshape(1, 1, MEM, H, HD),
            r["mv"].transpose(1, 0, 2).reshape(1, 1, MEM, H, HD))
```
